# Optimizing a Trainium2 kernel written in Bass

```python
import math
import jax, jax.numpy as jnp
from jax import lax
import numpy as np

D_MODEL = 1024
BATCH = 1
SEQ = 512
DEPTH = 1

HEAD_DIM = 64
HEADS_PER_GROUP = 4
DILATION_GROUPS = ((128, 1), (512, 4), (2048, 16))
N_GROUPS = len(DILATION_GROUPS)
N_ATTN_HEADS = N_GROUPS * HEADS_PER_GROUP
ATTN_WIDTH = N_ATTN_HEADS * HEAD_DIM
ATTN_OUT_WIDTH = HEADS_PER_GROUP * HEAD_DIM
QUERY_BLOCK = 128
CONV_WIDTH = D_MODEL // 2
CONV_KERNEL = 31
N_BRANCHES = 2
SPLIT_POINTS = (ATTN_WIDTH, 2 * ATTN_WIDTH, 3 * ATTN_WIDTH, 3 * ATTN_WIDTH + 2 * CONV_WIDTH)
IN_COLS = 3 * ATTN_WIDTH + 2 * CONV_WIDTH + N_BRANCHES * D_MODEL
N_BUCKETS = 32
MAX_DISTANCE = 2048
N_EXPERTS = 16
N_EXPERT_GROUPS = 4
EXPERTS_PER_GROUP = N_EXPERTS // N_EXPERT_GROUPS
TOP_K = 2
D_FF_EXPERT = D_MODEL
MOE_BLOCK = 128
ALPHA = (2 * DEPTH) ** 0.25
BETA = (8 * DEPTH) ** -0.25
LN_EPS = 1e-5

kernel_name = "hybrid_dilated_attn_conformer_grouped_moe_deepnorm"

def layer_norm(x, g, b):
    xf = x.astype(jnp.float32)
    mu = xf.mean(-1, keepdims=True)
    var = jnp.square(xf - mu).mean(-1, keepdims=True)
    y = (xf - mu) * lax.rsqrt(var + LN_EPS) * g.astype(jnp.float32) + b.astype(jnp.float32)
    return y.astype(x.dtype)

def t5_bucket(dist):
    max_exact = N_BUCKETS // 2
    n = jnp.maximum(dist, 0)
    nf = jnp.maximum(n, 1).astype(jnp.float32)
    large = max_exact + (jnp.log(nf / max_exact) / math.log(MAX_DISTANCE / max_exact)
                         * (N_BUCKETS - max_exact)).astype(jnp.int32)
    large = jnp.minimum(large, N_BUCKETS - 1)
    return jnp.where(n < max_exact, n, large)

def dilated_group_attention(q, k, v, rel_bias, window, dilation):
    B, S, H, dh = q.shape
    r = dilation
    L = S // r
    W = window // r
    bq = math.gcd(L, QUERY_BLOCK)
    nb = L // bq
    bk = bq + W
    qb = q.reshape(B, nb, bq, r, H, dh)
    pad = ((0, 0), (W, 0), (0, 0), (0, 0), (0, 0))
    kp = jnp.pad(k.reshape(B, L, r, H, dh), pad)
    vp = jnp.pad(v.reshape(B, L, r, H, dh), pad)
    kidx = jnp.arange(nb)[:, None] * bq + jnp.arange(bk)[None, :]
    kb = kp[:, kidx]
    vb = vp[:, kidx]
    qi = jnp.arange(bq)[:, None]
    kj = jnp.arange(bk)[None, :]
    dist = qi + W - kj
    key_pos = (jnp.arange(nb) * bq)[:, None, None] + kj[None] - W
    valid = (dist >= 0) & (dist <= W) & (key_pos >= 0)
    bias = jnp.moveaxis(rel_bias[t5_bucket(dist * r)], -1, 0)
    s = jnp.einsum('bnqchd,bnkchd->bnchqk', qb, kb).astype(jnp.float32) * (dh ** -0.5)
    s = s + bias.astype(jnp.float32)
    s = jnp.where(valid[None, :, None, None], s, -jnp.inf)
    m = s.max(-1, keepdims=True)
    p = jnp.exp(s - m)
    den = p.sum(-1)
    o = jnp.einsum('bnchqk,bnkchd->bnqchd', p / den[..., None], vb.astype(jnp.float32))
    o = o.reshape(B, S, H, dh)
    lse = m[..., 0] + jnp.log(den)
    lse = jnp.transpose(lse, (0, 1, 4, 2, 3)).reshape(B, S, H)
    return o, lse

def conformer_conv(u, conv_w, conv_b, ln_g, ln_b, w_out):
    a, gate = jnp.split(u, 2, axis=-1)
    h = a * jax.nn.sigmoid(gate)
    h = lax.conv_general_dilated(h, conv_w[:, None, :], window_strides=(1,),
                                 padding=[(CONV_KERNEL - 1, 0)],
                                 dimension_numbers=('NWC', 'WIO', 'NWC'),
                                 feature_group_count=CONV_WIDTH) + conv_b
    h = jax.nn.silu(layer_norm(h, ln_g, ln_b))
    return h @ w_out

def gated_mixer(x, w_in, rel_bias, conv_w, conv_b, conv_ln_g, conv_ln_b, w_attn_out, w_conv_out, w_o):
    B, S, _ = x.shape
    proj = x @ w_in
    q, k, v, u, g = jnp.split(proj, list(SPLIT_POINTS), axis=-1)
    q = q.reshape(B, S, N_ATTN_HEADS, HEAD_DIM)
    k = k.reshape(B, S, N_ATTN_HEADS, HEAD_DIM)
    v = v.reshape(B, S, N_ATTN_HEADS, HEAD_DIM)
    outs, lses = [], []
    for gi, (window, dilation) in enumerate(DILATION_GROUPS):
        hs = slice(gi * HEADS_PER_GROUP, (gi + 1) * HEADS_PER_GROUP)
        o, lse = dilated_group_attention(q[:, :, hs], k[:, :, hs], v[:, :, hs],
                                         rel_bias[:, hs], window, dilation)
        outs.append(o)
        lses.append(lse)
    mix_w = jax.nn.softmax(jnp.stack(lses), axis=0)
    attn = jnp.einsum('gbsh,gbshd->bshd', mix_w, jnp.stack(outs))
    attn = attn.reshape(B, S, ATTN_OUT_WIDTH).astype(x.dtype)
    attn_branch = attn @ w_attn_out
    conv_branch = conformer_conv(u, conv_w, conv_b, conv_ln_g, conv_ln_b, w_conv_out)
    gates = jax.nn.sigmoid(g.astype(jnp.float32)).astype(x.dtype).reshape(B, S, N_BRANCHES, D_MODEL)
    merged = gates[:, :, 0] * attn_branch + gates[:, :, 1] * conv_branch
    return merged @ w_o

def grouped_moe(x2d, router_w, w_gu, w_dn):
    N, D = x2d.shape
    probs = jax.nn.softmax((x2d @ router_w).astype(jnp.float32), axis=-1)
    grp = probs.reshape(N, N_EXPERT_GROUPS, EXPERTS_PER_GROUP)
    group_score = lax.top_k(grp, TOP_K)[0].sum(-1)
    g_sel = jnp.argmax(group_score, axis=-1)
    in_group = jnp.take_along_axis(grp, g_sel[:, None, None], axis=1)[:, 0]
    top_vals, top_local = lax.top_k(in_group, TOP_K)
    expert_idx = g_sel[:, None] * EXPERTS_PER_GROUP + top_local
    gate_w = top_vals / top_vals.sum(-1, keepdims=True)
    n_slots = N * TOP_K
    e_flat = expert_idx.reshape(-1).astype(jnp.int32)
    tok = jnp.arange(n_slots) // TOP_K
    counts = jnp.zeros((N_EXPERTS,), jnp.int32).at[e_flat].add(1)
    padded = (counts + MOE_BLOCK - 1) // MOE_BLOCK * MOE_BLOCK
    pad_end = jnp.cumsum(padded)
    pad_start = pad_end - padded
    cnt_start = jnp.cumsum(counts) - counts
    order = jnp.argsort(e_flat, stable=True)
    sorted_e = e_flat[order]
    rank = jnp.arange(n_slots) - cnt_start[sorted_e]
    dest = jnp.zeros((n_slots,), jnp.int32).at[order].set((pad_start[sorted_e] + rank).astype(jnp.int32))
    n_blocks = -(-(n_slots + N_EXPERTS * (MOE_BLOCK - 1)) // MOE_BLOCK)
    buf = jnp.zeros((n_blocks * MOE_BLOCK, D), x2d.dtype).at[dest].set(x2d[tok])
    block_e = jnp.minimum(jnp.searchsorted(pad_end, jnp.arange(n_blocks) * MOE_BLOCK, side='right'),
                          N_EXPERTS - 1)

    def expert_block(args):
        xb, e = args
        a, b = jnp.split(xb @ w_gu[e], 2, axis=-1)
        return (jax.nn.silu(a) * b) @ w_dn[e]

    y_buf = lax.map(expert_block, (buf.reshape(n_blocks, MOE_BLOCK, D), block_e)).reshape(-1, D)
    y_slots = y_buf[dest].reshape(N, TOP_K, D)
    return jnp.einsum('nk,nkd->nd', gate_w.astype(x2d.dtype), y_slots)

def setup_inputs(seed: int = 0) -> dict:
    key = jax.random.key(seed)
    ks = jax.random.split(key, 18)
    f32 = jnp.float32

    def nrm(k, shape, fan_in, scale=1.0):
        return jax.random.normal(k, shape, f32) * (scale * fan_in ** -0.5)

    def gain(k, shape):
        return 1.0 + 0.02 * jax.random.normal(k, shape, f32)

    def small(k, shape):
        return 0.02 * jax.random.normal(k, shape, f32)

    x = jax.random.normal(ks[0], (BATCH, SEQ, D_MODEL), f32)
    w_in = nrm(ks[1], (DEPTH, D_MODEL, IN_COLS), D_MODEL)
    w_in = w_in.at[..., 2 * ATTN_WIDTH:3 * ATTN_WIDTH].multiply(BETA)
    return {
        "x": x,
        "w_in": w_in,
        "w_attn_out": nrm(ks[2], (DEPTH, ATTN_OUT_WIDTH, D_MODEL), ATTN_OUT_WIDTH),
        "w_conv_out": nrm(ks[3], (DEPTH, CONV_WIDTH, D_MODEL), CONV_WIDTH),
        "w_o": nrm(ks[4], (DEPTH, D_MODEL, D_MODEL), D_MODEL, BETA),
        "conv_w": nrm(ks[5], (DEPTH, CONV_KERNEL, CONV_WIDTH), CONV_KERNEL),
        "conv_b": small(ks[6], (DEPTH, CONV_WIDTH)),
        "conv_ln_g": gain(ks[7], (DEPTH, CONV_WIDTH)),
        "conv_ln_b": small(ks[8], (DEPTH, CONV_WIDTH)),
        "ln_mix_g": gain(ks[9], (DEPTH, D_MODEL)),
        "ln_mix_b": small(ks[10], (DEPTH, D_MODEL)),
        "expert_w_gate_up": nrm(ks[11], (DEPTH, N_EXPERTS, D_MODEL, 2 * D_FF_EXPERT), D_MODEL, BETA),
        "expert_w_down": nrm(ks[12], (DEPTH, N_EXPERTS, D_FF_EXPERT, D_MODEL), D_FF_EXPERT, BETA),
        "ln_ffn_g": gain(ks[13], (DEPTH, D_MODEL)),
        "ln_ffn_b": small(ks[14], (DEPTH, D_MODEL)),
        "router_w": nrm(ks[15], (D_MODEL, N_EXPERTS), D_MODEL),
        "rel_bias": 0.5 * jax.random.normal(ks[16], (N_BUCKETS, N_ATTN_HEADS), f32),
    }

def reference(x, w_in, w_attn_out, w_conv_out, w_o, conv_w, conv_b, conv_ln_g, conv_ln_b,
              ln_mix_g, ln_mix_b, expert_w_gate_up, expert_w_down, ln_ffn_g, ln_ffn_b,
              router_w, rel_bias):
    B, S, D = x.shape
    for l in range(DEPTH):
        h = gated_mixer(x, w_in[l], rel_bias, conv_w[l], conv_b[l], conv_ln_g[l], conv_ln_b[l],
                        w_attn_out[l], w_conv_out[l], w_o[l])
        x = layer_norm(ALPHA * x + h, ln_mix_g[l], ln_mix_b[l])
        m = grouped_moe(x.reshape(B * S, D), router_w, expert_w_gate_up[l], expert_w_down[l])
        x = layer_norm(ALPHA * x + m.reshape(B, S, D), ln_ffn_g[l], ln_ffn_b[l])
    return x


_drawn_inputs = setup_inputs


def setup_inputs(seed=0):
    import zlib

    import numpy as np

    out = dict(_drawn_inputs(seed))
    spreads = {}
    factors = {'conv_b': 6.404,
     'conv_ln_g': 25.363,
     'conv_ln_b': 64.631,
     'ln_ffn_g': 20.876,
     'ln_ffn_b': 21.752,
     'rel_bias': 20.761,
     'ln_mix_b': 2.702,
     'w_attn_out': 3.86}
    for name, (base, spread) in spreads.items():
        noise = np.random.default_rng([zlib.crc32(name.encode()), seed]).standard_normal(out[name].shape)
        drawn = base * np.exp(spread * noise) if base else spread * noise
        out[name] = __import__('jax').numpy.asarray(drawn.astype(out[name].dtype))
    for name, factor in factors.items():
        out[name] = (out[name] * factor).astype(out[name].dtype)
    return out
```

```python
from contextlib import ExitStack
import math

import numpy as np

import concourse.bass as bass
from concourse import mybir

F32 = mybir.dt.float32
F32R = mybir.dt.float32r
I32 = mybir.dt.int32
ALU = mybir.AluOpType
ACT = mybir.ActivationFunctionType
AX = mybir.AxisListType

P = 128
D = 1024
S = 512
NT = S // P
KT = D // P
HD = 64
NG = 3
DIL = (1, 4, 16)
HPG = 4
GW = HPG * HD
AW = NG * GW
CW = D // 2
CT = CW // P
TAPS = 31
NBUCKET = 32
MAXDIST = 2048
NE = 16
EG = 4
FF = D
IN_COLS = 3 * AW + 2 * CW + 2 * D
ALPHA = 2.0 ** 0.25
EPS = 1e-5
NEG = -1.0e30
GTW = 384

CH = 2048
CC = CH // KT
RM, HM = 3, 2
RE, HE = 6, 3
GU, DN = 8, 4
MAXBLK = 24
TAB = 32


def mixer_chunks():
    q0, k0, v0, u0, g0 = 0, AW, 2 * AW, 3 * AW, 3 * AW + 2 * CW
    out = []
    for half in range(2):
        out += [("in", u0 + half * CC), ("in", u0 + CW + half * CC)]
    for g in range(NG):
        out += [("in", q0 + g * GW), ("in", k0 + g * GW), ("in", v0 + g * GW)]
    out += [("in", g0 + D + c * CC) for c in range(4)]
    out += [("in", g0 + c * CC) for c in range(4)]
    out += [("conv", 0), ("conv", 1), ("attn", 0)]
    out += [("o", c) for c in range(4)]
    return out


CHUNKS = mixer_chunks()
NM = len(CHUNKS)

U_STEPS = range(0, 8)
QKV_STEPS = range(8, 26)
G1_STEPS = range(26, 34)
G0_STEPS = range(34, 42)
CONV_STEPS = range(42, 50)
ATTN_STEPS = range(50, 58)
UNITS = NG * NT
UNIT_STEP = [14 + u if u < 4 else 20 + u - 4 if u < 8 else 26 + u - 8 for u in range(UNITS)]
STEP_UNIT = {s: u for u, s in enumerate(UNIT_STEP)}


def chunk_of_step(s):
    if s < 42:
        return s // 2, s % 2 == 0, s % 2 == 1
    if s < 50:
        return 21 + (s - 42) // 4, (s - 42) % 4 == 0, (s - 42) % 4 == 3
    return 23, s == 50, s == 57


def conv_plan():
    quota = {s: 4 for s in range(4, 8)}
    quota.update({s: 6 for s in range(8, 14)})
    quota.update({s: 4 for s in range(14, 26)})
    quota.update({s: 4 for s in range(26, 34)})
    ops = [(j, k) for pair in range(2) for k in range(TAPS) for j in (2 * pair, 2 * pair + 1)]
    plan, at = {}, 0
    for s in range(4, 34):
        n = quota[s]
        if s < 8:
            n = min(n, 2 * TAPS - at)
        plan[s] = ops[at:at + n]
        at += len(plan[s])
    plan[33] = plan[33] + ops[at:]
    return plan


CONV_PLAN = conv_plan()
STEP_END = [s for s in range(58) if chunk_of_step(s)[2]]


def tokens(row, g, i):
    return row[..., i * P:(i + 1) * P] if g == 0 else row[..., i::4]


def build(nc, x, w_in, w_attn_out, w_conv_out, w_o, conv_w, conv_b, conv_ln_g, conv_ln_b,
          ln_mix_g, ln_mix_b, expert_w_gate_up, expert_w_down, ln_ffn_g, ln_ffn_b, router_w,
          rel_bias, c_square, c_bucket, out):
    ctx = ExitStack()
    with ctx:
        base = (nc.sbuf_base + 63) // 64 * 64
        KB = 1024

        def at(name, shape, dt, kb):
            return nc.alloc_sbuf_tensor_at(name, shape, dt, offset=base + int(kb * KB)).ap()

        def sem(name):
            return ctx.enter_context(nc.semaphore(name))

        xh = at("xh", [P, KT, S], F32R, 0)
        xl = at("xl", [P, KT, S], F32R, 16)
        raw_m = [at(f"raw_m{s}", [P, CH], F32, 32 + 8 * s) for s in range(RM)]
        hi_m = [at(f"hi_m{s}", [P, CH], F32R, 56 + 8 * s) for s in range(HM)]
        lo_m = [at(f"lo_m{s}", [P, CH], F32R, 72 + 8 * s) for s in range(HM)]
        qk = at("qk", [P, 2, 2, 2, S], F32, 88)
        sg0 = at("sg0", [P, KT, S], F32, 88)
        x1 = at("x1", [P, NT, D], F32, 88)
        vv = at("vv", [P, 2, NT, GW], F32, 104)
        bm = at("bm", [P, 2, 2, 2 * P], F32, 112)
        bm12 = at("bm12", [P, 2, 2, 2, P], F32, 116)
        sc = at("sc", [P, 2, 2, 2, 2 * P], F32, 120)
        glu = at("glu", [P, 2, S], F32, 120)
        aTh = at("aTh", [P, 2, S], F32R, 120)
        aTl = at("aTl", [P, 2, S], F32R, 124)
        pT = at("pT", [P, 2 * S], F32, 128)
        oT = at("oT", [P, NG, 2, S], F32, 132)
        sg1 = at("sg1", [P, KT, S], F32, 144)
        xt = at("xt", [P, NT, D], F32, 144)
        hg = at("hg", [P, CT, S + TAPS - 1], F32, 160)
        ctm = at("ctm", [P, NT, CW], F32, 160)
        cacc = at("cacc", [P, CT, S], F32, 168.5)
        ch = at("ch", [P, CT, S], F32R, 168.5)
        cl = at("cl", [P, CT, S], F32R, 176.5)
        cwt_rows = at("cwt_rows", [TAPS + 3, CW], F32, 132)
        btab = at("btab", [NBUCKET + 1, NG, GTW], F32, 176.5)
        gsb = at("gsb", [HPG, NG, GTW], F32, 181.5)
        lnm = at("lnm", [P, 2, D], F32, 186.5)
        lnf = at("lnf", [P, 2, D], F32, 24)
        csil = at("csil", [P, 2, S], F32, 128)
        raw_e = raw_m + [at(f"raw_e{s}", [P, CH], F32, kb) for s, kb in ((3, 144), (4, 152), (5, 160))]
        hi_e = hi_m + [at("hi_e2", [P, CH], F32R, 136)]
        lo_e = lo_m + [at("lo_e2", [P, CH], F32R, 168.5)]
        xe = at("xe", [P, D], F32, 104)
        xeh = at("xeh", [P, KT, P], F32R, 108)
        xel = at("xel", [P, KT, P], F32R, 112)
        he = at("he", [P, FF], F32, 116)
        heh = at("heh", [P, KT, P], F32R, 120)
        hel = at("hel", [P, KT, P], F32R, 124)
        pe_sel = at("pe_sel", [P, NT, P], F32, 128)
        ye = at("ye", [P, D], F32, 132)
        x1T = [at("x1T0", [P, D], F32, 128), at("x1T1", [P, D], F32, 132)]
        yt = [at(f"yt{b}", [P, 2, D], F32, 8 * b) for b in range(2)]
        ot = [at(f"ot{b}", [P, D], F32, 16 + 4 * b) for b in range(2)]

        small = [194.5]

        def tiny(name, shape, dt=F32):
            n = int(np.prod(shape[1:])) * 4
            t = at(name, shape, dt, small[0])
            small[0] += (n + 31) // 32 * 32 / KB
            return t

        ident = tiny("ident", [P, P])
        upper = tiny("upper", [P, P])
        ones = tiny("ones", [P, P])
        iota = tiny("iota", [P, P])
        cwt = tiny("cwt", [P, CT, TAPS + 3])
        relb = tiny("relb", [NBUCKET + 1, NG * HPG])
        rw = tiny("rw", [P, KT, NE])
        cst = tiny("cst", [P, 64])
        nmx = tiny("nmx", [P, UNITS, HPG])
        den = tiny("den", [P, UNITS, HPG])
        rden = tiny("rden", [P, UNITS, HPG])
        lse = tiny("lse", [P, UNITS, HPG])
        stats = tiny("stats", [P, NT, 2, 6])
        mv = tiny("mv", [P, NT, 2])
        sd = tiny("sd", [P, NT, 1])
        nw = tiny("nw", [P, NT, 1])
        rstd = tiny("rstd", [P, NT, 2])
        spair = tiny("selpair", [HPG, 2, P])
        lg = tiny("lg", [P, NT, NE])
        pr = tiny("pr", [P, NT, NE])
        t16a = tiny("t16a", [P, NT, NE])
        t16b = tiny("t16b", [P, NT, NE])
        s6 = tiny("s6", [P, NT * EG, 6])
        gsc = tiny("gsc", [P, NT, EG])
        gcd = tiny("gcd", [P, NT, EG])
        ohg = tiny("ohg", [P, NT, EG])
        oh1 = tiny("oh1", [P, NT, NE])
        oh2 = tiny("oh2", [P, NT, NE])
        sel = tiny("sel", [P, NT, NE])
        c4 = tiny("c4", [P, 8, NT])
        gwt = tiny("gwt", [P, 2, NT])
        vt = tiny("vt", [P, NE, NT, 3])
        cnt = tiny("cnt", [P, NE])
        xtr = tiny("xtr", [P, NE])
        cs = tiny("cs", [P, 2, NE])
        ov = tiny("ov", [P, 8, NE])
        ov2 = tiny("ov2", [P, 8, NE])
        bbase = tiny("bbase", [P, TAB])
        etf = tiny("etf", [P, TAB])
        eti = tiny("eti", [P, TAB], I32)
        blk = tiny("blk", [P, NT, 3])
        idf = tiny("idf", [P, 2])
        idz = tiny("idz", [P, 2])
        gidx = tiny("gidx", [P, 1], I32)
        sidx = [tiny(f"sidx{s}", [P, 1], I32) for s in range(3)]
        lsT = at("lsT", [HPG, NG, S], F32, 112)
        mxT = at("mxT", [HPG, S], F32, 118)
        assert base + small[0] * KB <= nc.sbuf_usable_end, small

        ps = ctx.enter_context(nc.psum_tensor("ps", [P, 8, S], F32)).ap()

        gtab = nc.dram_tensor("gtab", [NG * HPG, P, GTW], F32).ap()
        x1d = nc.dram_tensor("x1d", [S, D], F32).ap()
        yd = nc.dram_tensor("yd", [2 * S, D], F32).ap()

        raw_in = [sem(f"raw_in{s}") for s in range(RE)]
        hi_ready, lo_ready = sem("hi_ready"), sem("lo_ready")
        chunk_used = sem("chunk_used")
        x_in, sq_in, tab_in, cw_in, ln_in, small_in = (sem(n) for n in
                                                       ("x_in", "sq_in", "tab_in", "cw_in", "ln_in", "small_in"))
        relb_one, pad_zero = sem("relb_one"), sem("pad_zero")
        cw_T, cw_ready = sem("cw_T"), sem("cw_ready")
        xT_done, xh_ready, xl_ready = sem("xT_done"), sem("xh_ready"), sem("xl_ready")
        gt_mm, gt_sb, gt_out, bm_in = sem("gt_mm"), sem("gt_sb"), sem("gt_out"), sem("bm_in")
        proj_done, proj_evac = sem("proj_done"), sem("proj_evac")
        glu_sig, glu_done = sem("glu_sig"), sem("glu_done")
        conv_op = sem("conv_op")
        att_s, s_add, s_max, att_exp, r_den, att_p = (sem(n) for n in
                                                      ("att_s", "s_add", "s_max", "att_exp", "r_den", "att_p"))
        att_t, pt_evac, att_o, o_evac = sem("att_t"), sem("pt_evac"), sem("att_o"), sem("o_evac")
        ln_den, lse_ready, lse_T, mixv, mix_exp, mix_F, mixc, aT_sum, aT_hi, aT_ready = (
            sem(n) for n in ("ln_den", "lse_ready", "lse_T", "mixv", "mix_exp", "mix_F", "mixc", "aT_sum", "aT_hi",
                             "aT_ready"))
        cT_done, cstat, cnorm, cb_T, c_silu, c_hi, c_ready = (
            sem(n) for n in ("cT_done", "cstat", "cnorm", "cb_T", "c_silu", "c_hi", "c_ready"))
        sig1, sig0 = sem("sig1"), sem("sig0")
        mcv, mga, merged_sum, m_hi, m_ready = (sem(n) for n in ("mcv", "mga", "merged_sum", "m_hi", "m_ready"))
        xr_in, wo_done, wo_used, lnv, ln1_norm, x1_ready, x1_out = (
            sem(n) for n in ("xr_in", "wo_done", "wo_used", "lnv", "ln1_norm", "x1_ready", "x1_out"))
        x1_T, x1T_sb, logits, rv, r_exp, sel_ready, rank_mm, tables = (
            sem(n) for n in ("x1_T", "x1T_sb", "logits", "rv", "r_exp", "sel_ready", "rank_mm", "tables"))
        newton = sem("newton")
        gathers_begun, scatters_begun = sem("gathers_begun"), sem("scatters_begun")
        xe_zero, ones_set, lnf_in = sem("xe_zero"), sem("ones_set"), sem("lnf_in")
        bv, idv, sel_blk, idx_mm, idx_ready, xe_in, xe_T, xeh_ready, xel_ready = (
            sem(n) for n in ("bv", "idv", "sel_blk", "idx_mm", "idx_ready", "xe_in", "xe_T", "xeh_ready", "xel_ready"))
        silu_done, he_ready, he_T, heh_ready, hel_ready, ye_ready, y_out = (
            sem(n) for n in ("silu_done", "he_ready", "he_T", "heh_ready", "hel_ready",
                             "ye_ready", "y_out"))
        yt_in = [sem("yt_in0"), sem("yt_in1")]
        fin_s, fin_a, fv, fin_norm, fin_ready, gv, lgv, crstd, lrstd, frstd, csd, lsd, fsd = (
            sem(n) for n in ("fin_s", "fin_a", "fv", "fin_norm", "fin_ready", "gv", "lgv", "crstd", "lrstd", "frstd", "csd", "lsd", "fsd"))
        out_st = [sem("out_st0"), sem("out_st1")]

        win_v = w_in.rearrange("a (k p) c -> p (a k) c", p=P)
        wco_v = w_conv_out.rearrange("a (k p) c -> p (a k) c", p=P)
        wao_v = w_attn_out.rearrange("a (k p) c -> p (a k) c", p=P)
        wo_v = w_o.rearrange("a (k p) c -> p (a k) c", p=P)
        wgu_v = expert_w_gate_up.rearrange("a e (k p) c -> (a e) k p c", p=P)
        wdn_v = expert_w_down.rearrange("a e (c k p) n -> (a e) c p k n", p=P, k=2)
        x_v = x.rearrange("b (t p) d -> p (b t) d", p=P)
        out_v = out.rearrange("b (t p) d -> (b t) p d", p=P)
        x1d_v = x1d.rearrange("(t p) d -> t p d", p=P)
        yd_v = yd.rearrange("(t p k) d -> t p k d", p=P, k=2)

        def mixer_source(n):
            kind, c = CHUNKS[n]
            if kind == "in":
                return win_v[:, :, c:c + CC]
            if kind == "conv":
                return wco_v[:, :, c * 512:(c + 1) * 512]
            if kind == "attn":
                return wao_v
            return wo_v[:, 2 * c:2 * c + 2, :]

        def mixer_shape(tile, n):
            kind, _ = CHUNKS[n]
            k = {"in": KT, "conv": CT, "attn": 2, "o": 2}[kind]
            return tile.rearrange("p (k c) -> p k c", k=k)

        M_USES = [len(range(s, NM, RM)) for s in range(RM)] + [0] * (RE - RM)

        def landed(b, q):
            return b * 32 + 16 * (M_USES[q % RE] + q // RE + 1)

        block = ctx.enter_context(nc.Block())

        @block.sync
        def _(sp):
            for t in range(NT):
                sp.dma_start(xt[:, t], x_v[:, t]).then_inc(x_in, 16)
            for n in range(NM):
                if n >= RM:
                    sp.wait_ge(lo_ready, n - RM + 1)
                sp.dma_start(mixer_shape(raw_m[n % RM], n), mixer_source(n)).then_inc(raw_in[n % RM], 16)

            def load(b, q, src):
                if q >= RE:
                    sp.wait_ge(lo_ready, b * 12 + (NM + q - RE + 1))
                dst = raw_e[q % RE]
                if len(src.shape) == 3:
                    dst = dst.rearrange("p (k c) -> p k c", k=2)
                sp.dma_start(dst, src).then_inc(raw_in[q % RE], 16)

            def block_chunks(b, cur, prev):
                for c in range(GU):
                    load(b, GU + c, expert(wgu_v, cur)[c])
                for c in range(DN):
                    load(b, 2 * GU + c, expert(wdn_v, prev)[c])

            def expert(v, e):
                return v[e] if isinstance(e, int) else v[bass.ds(e, 1)].rearrange(
                    "a c p n -> (a c) p n" if len(v.shape) == 4 else "a c p k n -> (a c) p k n")

            for c in range(GU):
                if c < RM:
                    last = max(n for n in range(NM) if n % RM == c)
                    sp.wait_ge(lo_ready, last + 1)
                elif c == RM:
                    sp.wait_ge(m_ready, KT)
                load(0, c, wgu_v[0, c])
            with sp.Fori(1, NE) as i:
                block_chunks(i - 1, i, i - 1)
            sp.wait_ge(tables, 1)
            nblk = sp.value_load(eti[0:1, TAB - 1:TAB], min_val=0, max_val=MAXBLK - 1 - NE) + NE
            with sp.If(nblk > NE):
                with sp.Fori(NE, nblk) as i:
                    cur = sp.value_load(eti[0:1, bass.ds(i, 1)], min_val=0, max_val=NE - 1)
                    prev = sp.value_load(eti[0:1, bass.ds(i - 1, 1)], min_val=0, max_val=NE - 1)
                    block_chunks(i - 1, cur, prev)
            final = sp.value_load(eti[0:1, bass.ds(nblk - 1, 1)], min_val=0, max_val=NE - 1)
            for c in range(DN):
                load(nblk - 1, GU + c, expert(wdn_v, final)[c])
            sp.wait_ge(y_out, nblk * 16)
            for t in range(NT):
                if t >= 2:
                    sp.wait_ge(fin_a, t - 1)
                sp.dma_start(yt[t % 2], yd_v[t]).then_inc(yt_in[t % 2], 16)
                if t >= 1:
                    sp.wait_ge(fin_ready, t)
                    sp.dma_start(out_v[t - 1], ot[(t - 1) % 2]).then_inc(out_st[(t - 1) % 2], 16)
            sp.wait_ge(fin_ready, NT)
            sp.dma_start(out_v[NT - 1], ot[(NT - 1) % 2]).then_inc(out_st[(NT - 1) % 2], 16)
            sp.wait_ge(out_st[0], 32)
            sp.wait_ge(out_st[1], 32)

        @block.gpsimd
        def _(pool):
            pool.memset(ones, 1.0).then_inc(ones_set, 1)
            pool.dma_start(ident, c_square[0]).then_inc(sq_in, 16)
            pool.dma_start(cwt_rows[0:TAPS], conv_w[0]).then_inc(cw_in, 16)
            pool.dma_start(cwt_rows[TAPS:TAPS + 1], conv_b).then_inc(cw_in, 16)
            pool.dma_start(cwt_rows[TAPS + 1:TAPS + 2], conv_ln_g).then_inc(cw_in, 16)
            pool.dma_start(cwt_rows[TAPS + 2:TAPS + 3], conv_ln_b).then_inc(cw_in, 16)
            pool.dma_start(btab, c_bucket).then_inc(tab_in, 16)
            pool.dma_start(relb[0:NBUCKET], rel_bias).then_inc(tab_in, 16)
            pool.dma_start(upper, c_square[1]).then_inc(small_in, 16)
            pool.dma_start(iota, c_square[2]).then_inc(small_in, 16)
            pool.dma_start(cst, c_square[3, :, 0:64]).then_inc(small_in, 16)
            pool.dma_start(spair, c_square[4, 0:2 * HPG, :].rearrange("(h m) c -> h m c", m=2)).then_inc(small_in, 16)
            pool.dma_start(rw, router_w.rearrange("(k p) e -> p k e", p=P)).then_inc(small_in, 16)
            for j, v in enumerate((ln_mix_g, ln_mix_b)):
                pool.dma_start(lnm[:, j], bass.AP(v.tensor, 0, [[0, P], [1, D]])).then_inc(ln_in, 16)
            pool.wait_ge(gt_sb, NG)
            for g in range(NG):
                pool.dma_start(gtab[g * HPG:(g + 1) * HPG], bass.AP(gsb.tensor, gsb[:, g].offset,
                               [list(gsb.ap[0]), [0, P], [1, GTW]])).then_inc(gt_out, 16)
            pool.wait_ge(gt_out, 16 * NG)
            for a in range(2):
                pool.dma_start(bm[:, a], bass.AP(gtab.tensor, a * P * GTW + P - 1,
                                                     [[GTW - 1, P], [2 * P * GTW, 2], [1, 2 * P]])
                               ).then_inc(bm_in, 16)
                for g in (1, 2):
                    pool.dma_start(bm12[:, g - 1, a], bass.AP(gtab.tensor, (HPG * g + a) * P * GTW + 2 * P - 1,
                                                             [[GTW - 1, P], [2 * P * GTW, 2], [1, P]])).then_inc(bm_in, 16)
            pool.wait_ge(m_ready, KT)
            pool.dma_start(x1, x_v).then_inc(xr_in, 16)
            for t in range(NT):
                pool.wait_ge(x1_ready, t + 1)
                pool.dma_start(x1d_v[t], x1[:, t]).then_inc(x1_out, 16)
            for j, v in enumerate((ln_ffn_g, ln_ffn_b)):
                pool.dma_start(lnf[:, j], bass.AP(v.tensor, 0, [[0, P], [1, D]])).then_inc(lnf_in, 16)
            pool.wait_ge(x1_out, 16 * NT)
            pool.memset(xe, 0.0).then_inc(xe_zero, 1)

            def gather(i):
                pool.wait_ge(idx_ready, i + 1)
                pool.sem_inc(gathers_begun, 1)
                pool.indirect_dma_start(xe, None, x1d, bass.IndirectOffsetOnAxis(gidx[:, 0:1], 0),
                                        bounds_check=S - 1, oob_is_err=False).then_inc(xe_in, 16)

            def scatter(i, slot):
                pool.wait_ge(ye_ready, i + 1)
                pool.sem_inc(scatters_begun, 1)
                pool.indirect_dma_start(yd, bass.IndirectOffsetOnAxis(sidx[slot][:, 0:1], 0), ye, None,
                                        bounds_check=2 * S - 1, oob_is_err=False).then_inc(y_out, 16)

            pool.wait_ge(xe_zero, 1)
            gather(0)
            for i in range(2):
                pool.wait_ge(xe_T, i + 1)
                gather(i + 1)
            pool.wait_ge(tables, 1)
            nblk = pool.value_load(eti[0:1, TAB - 1:TAB], min_val=0, max_val=MAXBLK - 1 - NE) + NE
            with pool.Fori(2, nblk) as i:
                scatter(i - 2, 2)
                pool.wait_ge(xe_T, i + 1)
                gather(i + 1)
            for k in (2, 1):
                scatter(nblk - k, k)

        @block.tensor
        def _(pe):
            def three(dst, a, b, c, d, first, last):
                pe.matmul(dst, a, c, start=first, stop=False)
                pe.matmul(dst, a, d, start=False, stop=False)
                return pe.matmul(dst, b, c, start=False, stop=last)

            pe.wait_ge(sq_in, 16)
            pe.wait_ge(x_in, 16 * NT)
            for k in range(KT):
                for t in range(NT):
                    mm = pe.transpose(ps[:, k, t * P:(t + 1) * P], xt[:, t, k * P:(k + 1) * P], ident)
                mm.then_inc(xT_done, 1)
            pe.wait_ge(cw_in, 64)
            pe.wait_ge(xl_ready, 5)
            for j in range(CT):
                mm = pe.transpose(ps[:, 4, j * 64:j * 64 + TAPS + 3], cwt_rows[:, j * P:(j + 1) * P],
                                  ident[0:TAPS + 3, 0:TAPS + 3])
            mm.then_inc(cw_T, 1)
            pe.wait_ge(tab_in, 32)
            pe.wait_ge(relb_one, 1)
            for g in range(NG):
                pe.wait_ge(xl_ready, 6 + g)
                pe.matmul(ps[0:HPG, 5 + g, 0:GTW],
                          relb[:, HPG * g:HPG * (g + 1)],
                          btab[:, g], start=True, stop=True).then_inc(gt_mm, 1)

            def scores(u):
                g, i = divmod(u, NT)
                w = 2 * P if g == 0 and i > 0 else P
                pe.wait_ge(proj_evac, 6 * g + 4)
                if u >= 1:
                    pe.wait_ge(s_add, u)
                if u == 0:
                    pe.wait_ge(glu_done, CT)
                for a in range(2):
                    for m in range(2):
                        q = qk[a * HD:(a + 1) * HD, g % 2, 0, m]
                        k = qk[a * HD:(a + 1) * HD, g % 2, 1, m]
                        keys = k[:, (i - 1) * P:(i + 1) * P] if w > P else tokens(k, g, i)
                        mm = pe.matmul(ps[:, 2 + a, m * w:(m + 1) * w], tokens(q, g, i), keys, start=True, stop=True)
                mm.then_inc(att_s, 1)

            def transpose_probs(u):
                g, i = divmod(u, NT)
                w = 2 * P if g == 0 and i > 0 else P
                pe.wait_ge(att_p, u + 1)
                if u >= 1:
                    pe.wait_ge(pt_evac, u)
                for kt in range(w // P):
                    for a in range(2):
                        for m in range(2):
                            mm = pe.transpose(ps[:, 4 + kt, (2 * a + m) * P:(2 * a + m + 1) * P],
                                              sc[:, u % 2, a, m, kt * P:(kt + 1) * P], ident)
                mm.then_inc(att_t, 1)

            def weighted_values(u):
                g, i = divmod(u, NT)
                tiles = [i - 1, i] if g == 0 and i > 0 else [i]
                pe.wait_ge(pt_evac, u + 1)
                pe.wait_ge(proj_evac, 6 * g + 6)
                if u >= 1:
                    pe.wait_ge(o_evac, u)
                for a in range(2):
                    for m in range(2):
                        h = 2 * m + a
                        for n, kt in enumerate(tiles):
                            mm = pe.matmul(ps[a * HD:(a + 1) * HD, 6, m * P:(m + 1) * P],
                                           vv[:, g % 2, kt, h * HD:(h + 1) * HD],
                                           pT[:, n * S + (2 * a + m) * P:n * S + (2 * a + m + 1) * P],
                                           start=(n == 0), stop=(n == len(tiles) - 1))
                mm.then_inc(att_o, 1)

            for s in range(58):
                if s in STEP_UNIT:
                    scores(STEP_UNIT[s])
                if s - 1 in STEP_UNIT:
                    transpose_probs(STEP_UNIT[s - 1])
                if s - 2 in STEP_UNIT:
                    weighted_values(STEP_UNIT[s - 2])
                if s == 33:
                    pe.wait_ge(lse_ready, 1)
                    pe.wait_ge(pt_evac, UNITS)
                    for u in range(UNITS):
                        g, i = divmod(u, NT)
                        mm = pe.transpose(ps[0:HPG, 2 + g, i * P:(i + 1) * P], lse[:, u], ident)
                    mm.then_inc(lse_T, 1)
                if s == 35:
                    pe.wait_ge(conv_op, CT * TAPS)
                    pe.wait_ge(mixv, 3)
                    pe.wait_ge(o_evac, UNITS)
                    for t in range(NT):
                        for j in range(CT):
                            mm = pe.transpose(ps[:, 4 + t, j * P:(j + 1) * P], cacc[:, j, t * P:(t + 1) * P], ident)
                        mm.then_inc(cT_done, 1)
                if s == 37:
                    pe.wait_ge(cnorm, NT)
                    for j in range(CT):
                        for t in range(NT):
                            mm = pe.transpose(ps[:, 4 + j, t * P:(t + 1) * P], ctm[:, t, j * P:(j + 1) * P], ident)
                        mm.then_inc(cb_T, 1)
                if s == 39:
                    pe.wait_ge(mixv, 10)
                    pe.wait_ge(c_silu, CT)
                    for m in range(2):
                        for g in range(NG):
                            pe.matmul(ps[:, 2 + NG * m + g], spair[:, m], lsT[:, g], start=True, stop=True
                                      ).then_inc(mix_F, 1)
                n, first, last = chunk_of_step(s)
                if first:
                    pe.wait_ge(lo_ready, n + 1)
                h_, l_ = mixer_shape(hi_m[n % HM], n), mixer_shape(lo_m[n % HM], n)
                if s < 8:
                    bank = s
                    if s == 0:
                        pe.wait_ge(xl_ready, KT)
                    if s == 4:
                        pe.wait_ge(cw_ready, 1)
                    if 5 <= s:
                        pe.wait_ge(gt_sb, s - 4)
                else:
                    bank = s % 2
                    if s < 10:
                        pe.wait_ge(glu_done, s - 7)
                    elif s < 43:
                        pe.wait_ge(proj_evac, s - 9)
                    elif s < 44:
                        pe.wait_ge(proj_evac, 34)
                    elif s < 52:
                        pe.wait_ge(mcv, s - 43)
                    else:
                        pe.wait_ge(mga, s - 51)
                if s in QKV_STEPS and (s - 8) % 6 >= 4:
                    g, half = (s - 8) // 6, (s - 8) % 6 - 4
                    for q in range(2):
                        i = 2 * half + q
                        for k in range(KT):
                            mm = three(ps[:, bank, q * GW:(q + 1) * GW], tokens(xh[:, k], g, i), tokens(xl[:, k], g, i),
                                       h_[:, k], l_[:, k], k == 0, k == KT - 1)
                elif s < 42:
                    cols = slice((s % 2) * P, (s % 2 + 1) * P)
                    for k in range(KT):
                        mm = three(ps[:, bank], h_[:, k, cols], l_[:, k, cols], xh[:, k], xl[:, k],
                                   k == 0, k == KT - 1)
                elif s < 50:
                    if s == 42:
                        pe.wait_ge(c_ready, CT)
                    cols = slice((s - 42) % 4 * P, ((s - 42) % 4 + 1) * P)
                    for k in range(CT):
                        mm = three(ps[:, bank], h_[:, k, cols], l_[:, k, cols], ch[:, k], cl[:, k],
                                   k == 0, k == CT - 1)
                else:
                    if s == 50:
                        pe.wait_ge(aT_ready, 2)
                    cols = slice((s - 50) * P, (s - 49) * P)
                    for k in range(2):
                        mm = three(ps[:, bank], h_[:, k, cols], l_[:, k, cols], aTh[:, k], aTl[:, k],
                                   k == 0, k == 1)
                mm.then_inc(proj_done, 1)
            for c in range(4):
                n = 24 + c
                h_, l_ = mixer_shape(hi_m[n % HM], n), mixer_shape(lo_m[n % HM], n)
                pe.wait_ge(lo_ready, n + 1)
                pe.wait_ge(m_ready, 2 * c + 2)
                if c == 0:
                    pe.wait_ge(mixc, 8)
                for t in range(NT):
                    tok = slice(t * P, (t + 1) * P)
                    for half in range(2):
                        if c == 0 and t == 0:
                            pe.wait_ge(mga, 7 + half)
                        for k in range(2):
                            kk = 2 * c + k
                            col = slice(half * 512, (half + 1) * 512)
                            mm = three(ps[:, 2 * t + half], xh[:, kk, tok], xl[:, kk, tok], h_[:, k, col],
                                       l_[:, k, col], kk == 0, kk == KT - 1)
                    if c == 3:
                        mm.then_inc(wo_done, 1)
                if c < 3:
                    mm.then_inc(wo_used, 1)
            pe.wait_ge(small_in, 80)
            for t in range(NT):
                pe.wait_ge(x1_ready, t + 1)
                for k in range(KT):
                    mm = pe.transpose(ps[:, 2 * t + k // 4, k % 4 * P:(k % 4 + 1) * P], x1[:, t, k * P:(k + 1) * P], ident)
                mm.then_inc(x1_T, 1)
                pe.wait_ge(x1T_sb, t + 1)
                for k in range(KT):
                    mm = pe.matmul(ps[:, 2 * t, 0:NE], x1T[t % 2][:, k * P:(k + 1) * P], rw[:, k],
                                   start=(k == 0), stop=(k == KT - 1))
                mm.then_inc(logits, 1)
            pe.wait_ge(sel_ready, 1)
            pe.wait_ge(ones_set, 1)
            for t in range(NT):
                for b in range(t + 1):
                    mm = pe.matmul(ps[:, 1, t * NE:(t + 1) * NE], upper if b == t else ones, sel[:, b],
                                   start=(b == 0), stop=(b == t))
            for t in range(NT):
                mm = pe.matmul(ps[:, 3, 0:NE], ones, sel[:, t], start=(t == 0), stop=(t == NT - 1))
            mm.then_inc(rank_mm, 1)

            def lookup(i):
                pe.wait_ge(sel_blk, i + 1)
                for t in range(NT):
                    mm = pe.matmul(ps[:, 7, 0:2], pe_sel[:, t], blk[:, t, 0:2], start=(t == 0), stop=(t == NT - 1))
                mm.then_inc(idx_mm, 1)

            def transpose_rows(i):
                pe.wait_ge(xe_in, 16 * i + 16)
                for k in range(KT):
                    mm = pe.transpose(ps[:, 6 + k // 4, k % 4 * P:(k % 4 + 1) * P], xe[:, k * P:(k + 1) * P], ident)
                mm.then_inc(xe_T, 1)

            def gate_up(i, b, q0):
                pe.wait_ge(xel_ready, i + 1)
                pe.wait_ge(xeh_ready, i + 1)
                if q0:
                    pe.wait_ge(he_ready, i)
                for c in range(GU):
                    q = q0 + c
                    h_, l_ = hi_e[q % HE], lo_e[q % HE]
                    pe.wait_ge(lo_ready, b * 12 + (NM + q + 1))
                    for n, (rows, cols) in enumerate(((xeh, h_), (xeh, l_), (xel, h_))):
                        for k in range(4):
                            mm = pe.matmul(ps[:, k], rows[:, c], cols[:, k * 512:(k + 1) * 512],
                                           start=(c == 0 and n == 0), stop=(c == GU - 1 and n == 2))
                    mm.then_inc(chunk_used, 1)
                    if c == 3:
                        if q0:
                            pe.wait_ge(hel_ready, i)
                            pe.wait_ge(heh_ready, i)
                        lookup(i + 1)
                transpose_rows(i + 1)

            def down(i, b, q0, prev):
                pe.wait_ge(heh_ready, i + 1)
                pe.wait_ge(hel_ready, i + 1)
                if prev:
                    pe.wait_ge(ye_ready, i)
                for c in range(DN):
                    q = q0 + c
                    h_, l_ = hi_e[q % HE], lo_e[q % HE]
                    pe.wait_ge(lo_ready, b * 12 + (NM + q + 1))
                    for k in range(2):
                        for n, (rows, cols) in enumerate(((heh, h_), (heh, l_), (hel, h_))):
                            for half in range(2):
                                mm = pe.matmul(ps[:, 4 + half], rows[:, 2 * c + k],
                                               cols[:, k * D + half * 512:k * D + (half + 1) * 512],
                                               start=(c + k + n == 0), stop=(c == DN - 1 and k == 1 and n == 2))
                    mm.then_inc(chunk_used, 1)

            def transpose_hidden(i):
                pe.wait_ge(he_ready, i + 1)
                pe.wait_ge(xel_ready, i + 2)
                pe.wait_ge(xeh_ready, i + 2)
                for k in range(KT):
                    mm = pe.transpose(ps[:, 6 + k // 4, k % 4 * P:(k % 4 + 1) * P], he[:, k * P:(k + 1) * P], ident)
                mm.then_inc(he_T, 1)

            lookup(0)
            transpose_rows(0)
            gate_up(0, 0, 0)
            transpose_hidden(0)
            gate_up(1, 0, GU)
            down(0, 0, 2 * GU, False)
            transpose_hidden(1)
            pe.wait_ge(tables, 1)
            nblk = pe.value_load(eti[0:1, TAB - 1:TAB], min_val=0, max_val=MAXBLK - 1 - NE) + NE
            with pe.Fori(2, nblk) as i:
                gate_up(i, i - 1, GU)
                down(i - 1, i - 1, 2 * GU, True)
                transpose_hidden(i)
            down(nblk - 1, nblk - 1, GU, True)

        @block.scalar
        def _(act):
            def cut(n):
                act.wait_ge(raw_in[n % RM], 16 * (n // RM + 1))
                if HM <= n < 24 + HM:
                    act.wait_ge(proj_done, STEP_END[n - HM] + 1)
                elif n >= HM:
                    act.wait_ge(wo_used, n - HM - 23)
                act.activation(hi_m[n % HM], raw_m[n % RM], ACT.Copy).then_inc(hi_ready, 1)

            def deviation(t, wait, n, done):
                act.wait_ge(wait, n)
                act.activation(sd[:, t], mv[:, t, 1:2], ACT.Sqrt, bias=cst[:, 36:37]).then_inc(done, 1)

            cut(0)
            for k in range(KT):
                act.wait_ge(xT_done, k + 1)
                act.activation(xh[:, k], ps[:, k], ACT.Copy).then_inc(xh_ready, 1)
            act.wait_ge(cw_T, 1)
            act.activation(cwt, ps[:, 4, 0:64 * CT].rearrange("p (j k) -> p j k", k=64)[:, :, 0:TAPS + 3],
                           ACT.Copy).then_inc(cw_ready, 1)
            for g in range(NG):
                act.wait_ge(gt_mm, g + 1)
                act.activation(gsb[:, g], ps[0:HPG, 5 + g, 0:GTW], ACT.Copy).then_inc(gt_sb, 1)

            def evacuate(s):
                act.wait_ge(proj_done, s + 1)
                if s in U_STEPS:
                    if s % 4 >= 2:
                        c = s // 4 * 2 + s % 4 - 2
                        if c >= 2:
                            act.wait_ge(glu_done, c - 1)
                        act.activation(glu[:, c % 2], ps[:, s], ACT.Sigmoid).then_inc(glu_sig, 1)
                elif s in QKV_STEPS:
                    g, r = divmod(s - 8, 6)
                    if g == 2 and r == 0:
                        act.wait_ge(att_s, NT)
                    if g == 2 and r == 4:
                        act.wait_ge(att_o, NT)
                    if r < 4:
                        act.activation(qk[:, g % 2, r // 2, r % 2], ps[:, s % 2], ACT.Copy,
                                       scale=HD ** -0.5 if r < 2 else 1.0).then_inc(proj_evac, 1)
                    else:
                        act.activation(vv[:, g % 2, 2 * (r - 4):2 * (r - 4) + 2],
                                       ps[:, s % 2].rearrange("p (i c) -> p i c", i=2), ACT.Copy).then_inc(proj_evac, 1)
                elif s in G1_STEPS:
                    act.activation(sg1[:, s - 26], ps[:, s % 2], ACT.Copy).then_inc(proj_evac, 1)
                elif s in G0_STEPS:
                    if s == 34:
                        act.wait_ge(att_s, UNITS)
                    act.activation(sg0[:, s - 34], ps[:, s % 2], ACT.Copy).then_inc(proj_evac, 1)

            def exponentials(u):
                g, i = divmod(u, NT)
                w = 2 * P if g == 0 and i > 0 else P
                act.wait_ge(s_max, u + 1)
                for a in range(2):
                    for m in range(2):
                        h = 2 * a + m
                        e = act.activation(sc[:, u % 2, a, m, 0:w], sc[:, u % 2, a, m, 0:w], ACT.Exp,
                                           bias=nmx[:, u, h:h + 1], accum_out=den[:, u, h:h + 1])
                e.then_inc(att_exp, 1)

            def probs_T(u):
                g, i = divmod(u, NT)
                w = 2 if g == 0 and i > 0 else 1
                act.wait_ge(att_t, u + 1)
                if u >= 1:
                    act.wait_ge(att_o, u)
                act.activation(pT[:, 0:w * S], ps[:, 4:4 + w].rearrange("p a c -> p (a c)"), ACT.Copy).then_inc(pt_evac, 1)

            def outputs_T(u):
                g, i = divmod(u, NT)
                act.wait_ge(att_o, u + 1)
                if u == 0:
                    act.wait_ge(cw_ready, 1)
                src = ps[:, 6, 0:2 * P].rearrange("p (m c) -> p m c", m=2)
                act.activation(tokens(oT[:, g], g, i), src, ACT.Copy).then_inc(o_evac, 1)

            for s in range(58):
                n, first, last = chunk_of_step(s)
                if 1 <= s <= 42:
                    evacuate(s - 1)
                if s - 1 in STEP_UNIT:
                    probs_T(STEP_UNIT[s - 1])
                if s - 2 in STEP_UNIT:
                    outputs_T(STEP_UNIT[s - 2])
                if s in STEP_UNIT:
                    exponentials(STEP_UNIT[s])
                if first and n + 1 <= 24:
                    cut(n + 1)
                if s == 31:
                    act.wait_ge(r_den, UNITS)
                    act.activation(lse, den, ACT.Ln).then_inc(ln_den, 1)
                if s == 34:
                    act.wait_ge(mixv, 6)
                    act.activation(lsT, lsT, ACT.Exp).then_inc(mix_exp, 1)
                if s == 35:
                    act.wait_ge(small_in, 80)
                    for t in range(NT):
                        deviation(t, cstat, 2 * t + 2, csd)
                if s == 37:
                    for j in range(CT):
                        act.wait_ge(cb_T, j + 1)
                        if j >= 2:
                            act.wait_ge(c_ready, j - 1)
                        act.activation(csil[:, j % 2], ps[:, 4 + j], ACT.Silu, scale=cwt[:, j, TAPS + 1:TAPS + 2],
                                       bias=cwt[:, j, TAPS + 2:TAPS + 3]).then_inc(c_silu, 1)
                        act.wait_ge(c_silu, j + 1)
                        act.activation(ch[:, j], csil[:, j % 2], ACT.Copy).then_inc(c_hi, 1)
                if s == 39:
                    act.wait_ge(proj_evac, 26)
                    act.activation(sg1, sg1, ACT.Sigmoid).then_inc(sig1, 1)
                if s == 40:
                    for m in range(2):
                        act.wait_ge(aT_sum, m + 1)
                        act.activation(aTh[:, m], oT[:, 0, m], ACT.Copy).then_inc(aT_hi, 1)
                if s == 42:
                    act.wait_ge(proj_evac, 34)
                    act.activation(sg0, sg0, ACT.Sigmoid).then_inc(sig0, 1)
                if s >= 51:
                    act.wait_ge(merged_sum, s - 50)
                    act.activation(xh[:, s - 51], sg1[:, s - 51], ACT.Copy).then_inc(m_hi, 1)
            act.wait_ge(merged_sum, KT)
            act.activation(xh[:, KT - 1], sg1[:, KT - 1], ACT.Copy).then_inc(m_hi, 1)
            for n in range(25, NM):
                cut(n)
            for t in range(NT + 2):
                if t < NT:
                    deviation(t, lnv, 4 * t + 4, lsd)
                if 1 <= t <= NT:
                    act.wait_ge(lrstd, 4 * t)
                    act.activation(x1[:, t - 1], x1[:, t - 1], ACT.Identity, scale=rstd[:, t - 1, 0:1],
                                   bias=rstd[:, t - 1, 1:2]).then_inc(ln1_norm, 1)
                if t >= 2:
                    act.wait_ge(x1_T, t - 1)
                    act.activation(x1T[t % 2], ps[:, 2 * t - 4:2 * t - 2].rearrange("p a c -> p (a c)"), ACT.Copy
                                   ).then_inc(x1T_sb, 1)
            act.wait_ge(rv, 2)
            act.activation(pr, pr, ACT.Exp).then_inc(r_exp, 1)

            def cut_e(b, q):
                act.wait_ge(raw_in[q % RE], landed(b, q))
                if q >= HE:
                    act.wait_ge(chunk_used, b * 12 + (q - HE + 1))
                act.activation(hi_e[q % HE], raw_e[q % RE], ACT.Copy).then_inc(hi_ready, 1)

            def two_banks(bank):
                return ps[:, bank:bank + 2].rearrange("p a c -> p (a c)")

            def rows_hi(i):
                act.wait_ge(xe_T, i + 1)
                act.activation(xeh.rearrange("p k c -> p (k c)"), two_banks(6), ACT.Copy).then_inc(xeh_ready, 1)

            def hidden_hi(i):
                act.wait_ge(he_T, i + 1)
                act.activation(heh.rearrange("p k c -> p (k c)"), two_banks(6), ACT.Copy).then_inc(heh_ready, 1)

            def output(i, b, q):
                act.wait_ge(chunk_used, b * 12 + (q + 1))
                if not (isinstance(i, int) and i == 0):
                    act.wait_ge(y_out, i * 16)
                act.activation(ye, two_banks(4), ACT.Copy).then_inc(ye_ready, 1)

            def body(i, b, q0, n_chunks, skip=0, prev=True, prev2=True):
                for c in range(skip, n_chunks):
                    cut_e(b, q0 + c)
                    if c == 2 and prev:
                        hidden_hi(i - 1)
                        if prev2:
                            output(i - 2, b, q0 - 1)
                    if c == min(GU + 2, n_chunks - 1) and n_chunks > DN:
                        act.wait_ge(chunk_used, b * 12 + (q0 + GU))
                        act.activation(he, two_banks(0), ACT.Silu).then_inc(silu_done, 1)
                        rows_hi(i + 1)

            for m in range(HE):
                if m < 2:
                    act.wait_ge(wo_used, 3)
                    if m == 1:
                        act.wait_ge(wo_done, NT)
                cut_e(0, m)
            rows_hi(0)
            body(0, 0, 0, GU, skip=HE, prev=False)
            body(1, 0, GU, GU + DN, prev2=False)
            act.wait_ge(tables, 1)
            nblk = act.value_load(eti[0:1, TAB - 1:TAB], min_val=0, max_val=MAXBLK - 1 - NE) + NE
            body(2, 1, GU, GU + DN)
            with act.Fori(3, nblk) as i:
                body(i, i - 1, GU, GU + DN)
            body(nblk, nblk - 1, GU, DN)
            output(nblk - 1, nblk - 1, GU + DN - 1)
            for t in range(NT + 1):
                if t < NT:
                    act.wait_ge(yt_in[t % 2], 16 * (t // 2 + 1))
                    act.activation(yt[t % 2][:, 0], yt[t % 2][:, 0], ACT.Identity, scale=gwt[:, 0, t:t + 1]
                                   ).then_inc(fin_s, 1)
                    deviation(t, fv, 4 * t + 4, fsd)
                if t >= 1:
                    act.wait_ge(frstd, 4 * t)
                    act.activation(ot[(t - 1) % 2], ot[(t - 1) % 2], ACT.Identity, scale=rstd[:, t - 1, 0:1],
                                   bias=rstd[:, t - 1, 1:2]).then_inc(fin_norm, 1)

        @block.vector
        def _(dve):
            def cut(n):
                dve.wait_ge(hi_ready, n + 1)
                dve.tensor_tensor(lo_m[n % HM], raw_m[n % RM], hi_m[n % HM].bitcast(F32), ALU.subtract).then_inc(lo_ready, 1)

            def inverse(t, root, done):
                r = rstd[:, t, 0:1]
                dve.wait_ge(root, t + 1)
                dve.reciprocal(r, sd[:, t]).then_inc(newton, 1)
                dve.tensor_scalar(nw[:, t], mv[:, t, 1:2], EPS, None, ALU.add).then_inc(newton, 1)
                newton_at[0] += 2
                dve.wait_ge(newton, newton_at[0])
                dve.scalar_tensor_tensor(nw[:, t], nw[:, t], r, r, ALU.mult, ALU.mult).then_inc(done, 1)
                dve.wait_ge(done, 4 * t + 1)
                dve.tensor_scalar(nw[:, t], nw[:, t], -0.5, 1.5, ALU.mult, ALU.add).then_inc(done, 1)
                dve.wait_ge(done, 4 * t + 2)
                dve.tensor_tensor(r, r, nw[:, t], ALU.mult).then_inc(done, 1)
                dve.wait_ge(done, 4 * t + 3)
                dve.scalar_tensor_tensor(rstd[:, t, 1:2], mv[:, t, 0:1], -1.0, r, ALU.mult, ALU.mult).then_inc(done, 1)

            newton_at = [0]
            conv_at = [0]

            def conv(ops):
                for j, k in ops:
                    t = conv_at[0]
                    w = cwt[:, j, k:k + 1]
                    src = hg[:, j, k:k + S]
                    if k == 0:
                        dve.wait_ge(glu_done, j + 1)
                        dve.wait_ge(cw_ready, 1)
                        dve.wait_ge(pad_zero, 1)
                        dve.tensor_scalar(cacc[:, j], src, w, cwt[:, j, TAPS:TAPS + 1], ALU.mult, ALU.add).then_inc(conv_op, 1)
                    else:
                        dve.wait_ge(conv_op, t - 1)
                        dve.scalar_tensor_tensor(cacc[:, j], src, w, cacc[:, j], ALU.mult, ALU.add).then_inc(conv_op, 1)
                    conv_at[0] += 1

            dve.memset(hg[:, :, 0:TAPS - 1], 0.0).then_inc(pad_zero, 1)
            dve.memset(relb[NBUCKET:NBUCKET + 1], 1.0).then_inc(relb_one, 1)
            for k in range(KT):
                dve.wait_ge(xh_ready, k + 1)
                dve.tensor_tensor(xl[:, k], ps[:, k], xh[:, k].bitcast(F32), ALU.subtract).then_inc(xl_ready, 1)
                if k == 1:
                    cut(0)

            def add_bias(u):
                g, i = divmod(u, NT)
                w = 2 * P if g == 0 and i > 0 else P
                dve.wait_ge(att_s, u + 1)
                if u == 0:
                    dve.wait_ge(bm_in, 96)
                if u >= 2:
                    dve.wait_ge(att_t, u - 1)
                dst = sc[:, u % 2, :, :, 0:w]
                bias = bm12[:, g - 1] if g else bm if w > P else bm[:, :, :, P:2 * P]
                src = ps[:, 2:4, 0:2 * w].rearrange("p a (m w) -> p a m w", m=2)
                dve.tensor_tensor(dst, src, bias, ALU.add).then_inc(s_add, 1)
                dve.wait_ge(s_add, u + 1)
                dve.tensor_reduce(nmx[:, u].rearrange("p (a m) -> p a m", a=2), dst, AX.X, ALU.max, negate=True
                                  ).then_inc(s_max, 1)

            def normalise(u):
                g, i = divmod(u, NT)
                w = 2 * P if g == 0 and i > 0 else P
                dve.wait_ge(att_exp, u + 1)
                dve.reciprocal(rden[:, u], den[:, u]).then_inc(r_den, 1)
                dve.wait_ge(r_den, u + 1)
                v = sc[:, u % 2, :, :, 0:w]
                r = rden[:, u].rearrange("p (a m) -> p a m", a=2).unsqueeze(3).to_broadcast([P, 2, 2, w])
                dve.tensor_tensor(v, v, r, ALU.mult).then_inc(att_p, 1)

            mix_at = [0]

            def mix(ins):
                mix_at[0] += 1
                ins.then_inc(mixv, 1)
                dve.wait_ge(mixv, mix_at[0])

            def merge_lo(d):
                dve.wait_ge(m_hi, d + 1)
                dve.tensor_tensor(xl[:, d], sg1[:, d], xh[:, d].bitcast(F32), ALU.subtract).then_inc(m_ready, 1)

            for s in range(59):
                n, first, last = chunk_of_step(min(s, 57))
                if 1 <= s <= 8 and (s - 1) % 4 >= 2:
                    c = (s - 1) // 4 * 2 + (s - 1) % 4 - 2
                    dve.wait_ge(glu_sig, c + 1)
                    dve.tensor_tensor(hg[:, c, TAPS - 1:], ps[:, s - 3], glu[:, c % 2], ALU.mult).then_inc(glu_done, 1)
                if s in STEP_UNIT:
                    add_bias(STEP_UNIT[s])
                taps = CONV_PLAN.get(s, [])
                conv(taps[:len(taps) // 2])
                if s in STEP_UNIT:
                    normalise(STEP_UNIT[s])
                if s < 58 and first and n + 1 <= 24:
                    cut(n + 1)
                conv(taps[len(taps) // 2:])
                if s == 32:
                    dve.wait_ge(ln_den, 1)
                    dve.tensor_tensor(lse, lse, nmx, ALU.subtract).then_inc(lse_ready, 1)
                if s == 34:
                    dve.wait_ge(lse_T, 1)
                    mix(dve.tensor_copy(lsT[:, 0], ps[0:HPG, 2]))
                    for g in (1, 2):
                        mix(dve.tensor_copy(lsT[:, g].rearrange("h (l c) -> h c l", c=4),
                                            ps[0:HPG, 2 + g].rearrange("h (c l) -> h c l", c=4)))
                    mix(dve.tensor_tensor(mxT, lsT[:, 0], lsT[:, 1], ALU.max))
                    mix(dve.tensor_tensor(mxT, mxT, lsT[:, 2], ALU.max))
                    mix(dve.tensor_tensor(lsT, lsT, mxT.unsqueeze(1).to_broadcast([HPG, NG, S]), ALU.subtract))
                    dve.wait_ge(mix_exp, 1)
                    mix(dve.tensor_tensor(mxT, lsT[:, 0], lsT[:, 1], ALU.add))
                    mix(dve.tensor_tensor(mxT, mxT, lsT[:, 2], ALU.add))
                    mix(dve.reciprocal(mxT, mxT))
                    mix(dve.tensor_tensor(lsT, lsT, mxT.unsqueeze(1).to_broadcast([HPG, NG, S]), ALU.mult))
                if s == 35:
                    for t in range(NT):
                        dve.wait_ge(cT_done, t + 1)
                        dve.bn_stats(stats[:, t, 0], ps[:, 4 + t]).then_inc(cstat, 1)
                        dve.wait_ge(cstat, 2 * t + 1)
                        dve.bn_aggr(mv[:, t], stats[:, t, 0]).then_inc(cstat, 1)
                    for t in range(NT):
                        inverse(t, csd, crstd)
                        dve.wait_ge(crstd, 4 * t + 4)
                        dve.tensor_scalar(ctm[:, t], ps[:, 4 + t], mv[:, t, 0:1], rstd[:, t, 0:1], ALU.subtract, ALU.mult
                                          ).then_inc(cnorm, 1)
                if s == 37:
                    for j in range(CT):
                        dve.wait_ge(c_hi, j + 1)
                        dve.tensor_tensor(cl[:, j], csil[:, j % 2], ch[:, j].bitcast(F32), ALU.subtract).then_inc(c_ready, 1)
                if s == 39:
                    for m in range(2):
                        for g in range(NG):
                            dve.wait_ge(mix_F, NG * m + g + 1)
                            dve.tensor_tensor(oT[:, g, m], oT[:, g, m], ps[:, 2 + NG * m + g], ALU.mult).then_inc(mixc, 1)
                        dve.wait_ge(mixc, 4 * m + 3)
                        dve.tensor_tensor(oT[:, 0, m], oT[:, 0, m], oT[:, 1, m], ALU.add).then_inc(mixc, 1)
                        dve.wait_ge(mixc, 4 * m + 4)
                        dve.tensor_tensor(oT[:, 0, m], oT[:, 0, m], oT[:, 2, m], ALU.add).then_inc(aT_sum, 1)
                    for m in range(2):
                        dve.wait_ge(aT_hi, m + 1)
                        dve.tensor_tensor(aTl[:, m], oT[:, 0, m], aTh[:, m].bitcast(F32), ALU.subtract).then_inc(aT_ready, 1)
                if 43 <= s <= 50:
                    if s == 43:
                        dve.wait_ge(sig1, 1)
                    dve.wait_ge(proj_done, s)
                    dve.tensor_tensor(sg1[:, s - 43], sg1[:, s - 43], ps[:, (s - 1) % 2], ALU.mult).then_inc(mcv, 1)
                if s >= 51:
                    if s == 51:
                        dve.wait_ge(sig0, 1)
                    d = s - 51
                    dve.wait_ge(proj_done, s)
                    dve.tensor_tensor(sg0[:, d], sg0[:, d], ps[:, (s - 1) % 2], ALU.mult).then_inc(mga, 1)
                    dve.wait_ge(mga, d + 1)
                    dve.wait_ge(mcv, d + 1)
                    dve.tensor_tensor(sg1[:, d], sg1[:, d], sg0[:, d], ALU.add).then_inc(merged_sum, 1)
                    if d >= 1:
                        merge_lo(d - 1)
            merge_lo(KT - 1)
            for n in range(25, NM):
                cut(n)

            def gain(t, rows, par, norm, chain, done):
                dve.wait_ge(norm, t + 1)
                dve.tensor_tensor(rows, rows, par[:, 0], ALU.mult).then_inc(chain, 1)
                dve.wait_ge(chain, t + 1)
                dve.tensor_tensor(rows, rows, par[:, 1], ALU.add).then_inc(done, 1)

            def moments(t, rows, chain, at):
                dve.wait_ge(chain, at)
                for h in range(2):
                    dve.bn_stats(stats[:, t, h], rows[:, h * 512:(h + 1) * 512]).then_inc(chain, 1)
                dve.wait_ge(chain, at + 2)
                dve.bn_aggr(mv[:, t], stats[:, t]).then_inc(chain, 1)

            dve.wait_ge(ln_in, 32)
            dve.wait_ge(xr_in, 16)
            for t in range(NT + 2):
                if t < NT:
                    dve.wait_ge(wo_done, t + 1)
                    dve.scalar_tensor_tensor(x1[:, t], x1[:, t], ALPHA,
                                             ps[:, 2 * t:2 * t + 2].rearrange("p a c -> p (a c)"),
                                             ALU.mult, ALU.add).then_inc(lnv, 1)
                    moments(t, x1[:, t], lnv, 4 * t + 1)
                if 1 <= t <= NT:
                    inverse(t - 1, lsd, lrstd)
                if t >= 2:
                    gain(t - 2, x1[:, t - 2], lnm, ln1_norm, gv, x1_ready)

            rv_at = [0]

            def link(ins):
                rv_at[0] += 1
                ins.then_inc(rv, 1)
                dve.wait_ge(rv, rv_at[0])

            def over_e(v):
                return v.unsqueeze(2).to_broadcast([P, NT, NE])

            dve.wait_ge(small_in, 80)
            dve.wait_ge(logits, NT)
            lgp = ps[:, 0:8, 0:NE].rearrange("p (t a) e -> p t a e", a=2)[:, :, 0]
            link(dve.tensor_reduce(c4[:, 0], lgp, AX.X, ALU.max))
            link(dve.tensor_tensor(pr, lgp, over_e(c4[:, 0]), ALU.subtract))
            dve.wait_ge(r_exp, 1)
            link(dve.tensor_reduce(c4[:, 1], pr, AX.X, ALU.add))
            link(dve.reciprocal(c4[:, 1], c4[:, 1]))
            link(dve.tensor_tensor(pr, pr, over_e(c4[:, 1]), ALU.mult))
            p4 = pr.rearrange("p t (g e) -> p (t g) e", e=4)
            link(dve.tensor_tensor(s6[:, :, 0:3], p4[:, :, 0:3], p4[:, :, 1:4], ALU.add))
            link(dve.tensor_tensor(s6[:, :, 3:5], p4[:, :, 0:2], p4[:, :, 2:4], ALU.add))
            link(dve.tensor_tensor(s6[:, :, 5:6], p4[:, :, 0:1], p4[:, :, 3:4], ALU.add))
            link(dve.tensor_reduce(gsc.rearrange("p t g -> p (t g)"), s6, AX.X, ALU.max))

            def first_best(out_, vals, best, cand, n, ids, row):
                bc = lambda v: v.unsqueeze(2).to_broadcast([P, NT, n])
                link(dve.tensor_reduce(c4[:, row], vals, AX.X, ALU.max))
                link(dve.tensor_tensor(cand, vals, bc(c4[:, row]), ALU.is_ge))
                link(dve.scalar_tensor_tensor(cand, cand, -100.0, ids.unsqueeze(1).to_broadcast([P, NT, n]),
                                              ALU.mult, ALU.add))
                link(dve.tensor_reduce(c4[:, best], cand, AX.X, ALU.min))
                link(dve.tensor_tensor(out_, cand, bc(c4[:, best]), ALU.is_equal))

            ids16, ids4 = cst[:, 0:16], cst[:, 24:28]
            first_best(ohg, gsc, 3, gcd, EG, ids4, 2)
            og = ohg.rearrange("p t g -> p (t g)").unsqueeze(2).to_broadcast([P, NT * EG, 4])
            v16 = lambda v: v.rearrange("p t (g e) -> p (t g) e", e=4)
            link(dve.tensor_tensor(v16(t16a), p4, og, ALU.mult))
            link(dve.tensor_tensor(v16(t16a), v16(t16a), og, ALU.add))
            link(dve.tensor_scalar(t16a, t16a, -1.0, None, ALU.add))
            first_best(oh1, t16a, 3, t16b, NE, ids16, 4)
            link(dve.scalar_tensor_tensor(t16a, oh1, -4.0, t16a, ALU.mult, ALU.add))
            first_best(oh2, t16a, 3, t16b, NE, ids16, 5)
            link(dve.tensor_tensor(c4[:, 6], c4[:, 4], c4[:, 5], ALU.add))
            link(dve.reciprocal(c4[:, 6], c4[:, 6]))
            link(dve.tensor_tensor(gwt, c4[:, 4:6], c4[:, 6:7].to_broadcast([P, 2, NT]), ALU.mult))
            link(dve.tensor_tensor(sel, oh1, oh2, ALU.add))
            dve.engine_nop().then_inc(sel_ready, 1)
            vte = vt.rearrange("p e t c -> p t e c")
            link(dve.tensor_copy(vte[:, :, :, 0], cst[:, 16:20].unsqueeze(2).to_broadcast([P, NT, NE])))
            link(dve.tensor_tensor(vte[:, :, :, 1], oh2, cst[:, 20:24].unsqueeze(2).to_broadcast([P, NT, NE]), ALU.add))
            dve.wait_ge(rank_mm, 1)
            rk = ps[:, 1, 0:NT * NE].rearrange("p (t e) -> p t e", t=NT)
            link(dve.scalar_tensor_tensor(t16a, rk, 1.0, sel, ALU.add, ALU.mult))
            link(dve.tensor_scalar(vte[:, :, :, 2], t16a, -1.0, None, ALU.add))
            link(dve.tensor_copy(cnt, ps[:, 3, 0:NE]))
            link(dve.tensor_scalar(xtr, cnt, float(P), None, ALU.is_gt))
            for b in (2, 3):
                link(dve.scalar_tensor_tensor(xtr, cnt, float(b * P), xtr, ALU.is_gt, ALU.add))
            link(dve.tensor_copy(cs[:, 0], xtr))
            src = 0
            for sh in (1, 2, 4, 8):
                link(dve.tensor_copy(cs[:, 1 - src, 0:sh], cs[:, src, 0:sh]))
                link(dve.tensor_tensor(cs[:, 1 - src, sh:], cs[:, src, sh:], cs[:, src, :NE - sh], ALU.add))
                src = 1 - src
            link(dve.tensor_tensor(cs[:, 1 - src], cs[:, src], xtr, ALU.subtract))
            ends, starts = cs[:, src], cs[:, 1 - src]
            js = cst[:, 28:36].unsqueeze(2).to_broadcast([P, 8, NE])
            row = lambda v: v.unsqueeze(1).to_broadcast([P, 8, NE])
            link(dve.tensor_tensor(ov, js, row(ends), ALU.is_lt))
            link(dve.tensor_tensor(ov2, js, row(starts), ALU.is_ge))
            link(dve.tensor_tensor(ov, ov, ov2, ALU.mult))
            link(dve.tensor_tensor(ov2, js, row(starts), ALU.subtract))
            link(dve.scalar_tensor_tensor(ov2, ov2, 1.0, ov, ALU.add, ALU.mult))
            link(dve.memset(bbase, 0.0))
            link(dve.memset(etf, 0.0))
            link(dve.tensor_reduce(bbase[:, NE:NE + 8], ov2, AX.X, ALU.add))
            link(dve.tensor_scalar(bbase[:, NE:NE + 8], bbase[:, NE:NE + 8], float(P), None, ALU.mult))
            link(dve.tensor_tensor(ov, ov, row(ids16), ALU.mult))
            link(dve.tensor_reduce(etf[:, NE:NE + 8], ov, AX.X, ALU.add))
            link(dve.tensor_copy(etf[:, 0:NE], ids16))
            link(dve.tensor_copy(etf[:, TAB - 1:TAB], ends[:, NE - 1:NE]))
            dve.tensor_copy(eti, etf).then_inc(tables, 1)

            bv_at = [0]

            def select(i, static):
                if static:
                    e = i
                else:
                    e = dve.value_load(eti[0:1, bass.ds(i, 1)], min_val=0, max_val=NE - 1)
                dve.tensor_copy(blk, vt[:, bass.ds(e, 1)].rearrange("p a t c -> p (a t) c")).then_inc(bv, 1)
                dve.wait_ge(bv, i * 2 + 1)
                dve.tensor_scalar(blk[:, :, 2], blk[:, :, 2], bbase[:, bass.ds(i, 1)], None, ALU.subtract).then_inc(bv, 1)
                dve.wait_ge(bv, i * 2 + 2)
                for t in range(NT):
                    ins = dve.tensor_scalar(pe_sel[:, t], iota, blk[:, t, 2:3], None, ALU.is_equal)
                ins.then_inc(sel_blk, 1)

            def indices(i, shift, scattered):
                dve.wait_ge(idx_mm, i + 1)
                dve.tensor_copy(idf, ps[:, 7, 0:2]).then_inc(idv, 1)
                if scattered is not None:
                    dve.wait_ge(y_out, scattered * 16)
                if shift:
                    dve.tensor_copy(sidx[2], sidx[1]).then_inc(idv, 1)
                    dve.wait_ge(idv, i * 5 + 3)
                    dve.tensor_copy(sidx[1], sidx[0]).then_inc(idv, 1)
                    dve.wait_ge(idv, i * 5 + 4)
                else:
                    dve.memset(sidx[2], 0).then_inc(idv, 1)
                    dve.memset(sidx[1], 0).then_inc(idv, 1)
                    dve.memset(sidx[0], 0).then_inc(idv, 1)
                    dve.wait_ge(idv, 4)
                dve.tensor_scalar(idz, idf, 0.0, 8192.0, ALU.is_equal, ALU.mult).then_inc(idv, 1)
                dve.wait_ge(idv, i * 5 + 5)
                dve.scalar_tensor_tensor(idf, idf, -1.0, idz, ALU.add, ALU.add).then_inc(idv, 1)
                dve.wait_ge(idv, i * 5 + 6)
                dve.tensor_copy(sidx[0], idf[:, 1:2])
                dve.tensor_copy(gidx, idf[:, 0:1]).then_inc(idx_ready, 1)
                dve.wait_ge(idx_ready, i + 1)

            def rows_lo(i):
                dve.wait_ge(xeh_ready, i + 1)
                dve.tensor_tensor(xel.rearrange("p k c -> p (k c)"), ps[:, 6:8].rearrange("p a c -> p (a c)"),
                                  xeh.bitcast(F32).rearrange("p k c -> p (k c)"), ALU.subtract).then_inc(xel_ready, 1)

            def hidden_lo(i):
                dve.wait_ge(heh_ready, i + 1)
                dve.tensor_tensor(hel.rearrange("p k c -> p (k c)"), ps[:, 6:8].rearrange("p a c -> p (a c)"),
                                  heh.bitcast(F32).rearrange("p k c -> p (k c)"), ALU.subtract).then_inc(hel_ready, 1)

            def cut_e(b, q):
                dve.wait_ge(hi_ready, b * 12 + (NM + q + 1))
                dve.tensor_tensor(lo_e[q % HE], raw_e[q % RE], hi_e[q % HE].bitcast(F32), ALU.subtract).then_inc(lo_ready, 1)

            def body(i, b, q0, n_chunks, skip=0, prev=True, scattered=None):
                for c in range(skip, n_chunks):
                    cut_e(b, q0 + c)
                    if n_chunks > DN and c == max(1, skip):
                        select(i + 1, isinstance(i, int))
                    if c == 2 and prev:
                        hidden_lo(i - 1)
                    if n_chunks > DN and c == 6:
                        indices(i + 1, True, scattered)
                    if c == min(GU + 2, n_chunks - 1) and n_chunks > DN:
                        dve.wait_ge(silu_done, i + 1)
                        dve.tensor_tensor(he, he, ps[:, 2:4].rearrange("p a c -> p (a c)"), ALU.mult).then_inc(he_ready, 1)
                        rows_lo(i + 1)

            select(0, True)
            indices(0, False, None)
            for m in range(HE):
                cut_e(0, m)
            rows_lo(0)
            body(0, 0, 0, GU, skip=HE, prev=False)
            body(1, 0, GU, GU + DN)
            dve.wait_ge(tables, 1)
            nblk = dve.value_load(eti[0:1, TAB - 1:TAB], min_val=0, max_val=MAXBLK - 1 - NE) + NE
            with dve.Fori(2, nblk) as i:
                body(i, i - 1, GU, GU + DN, scattered=i - 1)
            body(nblk, nblk - 1, GU, DN)
            dve.wait_ge(lnf_in, 32)
            for t in range(NT):
                o = ot[t % 2]
                dve.wait_ge(fin_s, t + 1)
                if t >= 2:
                    dve.wait_ge(out_st[t % 2], 16)
                dve.scalar_tensor_tensor(o, yt[t % 2][:, 1], gwt[:, 1, t:t + 1], yt[t % 2][:, 0], ALU.mult, ALU.add
                                         ).then_inc(fin_a, 1)
                dve.wait_ge(fin_a, t + 1)
                dve.scalar_tensor_tensor(o, x1[:, t], ALPHA, o, ALU.mult, ALU.add).then_inc(fv, 1)
                moments(t, o, fv, 4 * t + 1)
                inverse(t, fsd, frstd)
                if t >= 1:
                    gain(t - 1, ot[(t - 1) % 2], lnf, fin_norm, lgv, fin_ready)
            gain(NT - 1, ot[(NT - 1) % 2], lnf, fin_norm, lgv, fin_ready)


def bucket(dist):
    exact = NBUCKET // 2
    if dist < exact:
        return dist
    v = np.log(np.float32(dist) / np.float32(exact)) / np.float32(math.log(MAXDIST / exact)) * np.float32(NBUCKET - exact)
    return min(exact + int(v), NBUCKET - 1)


def constants():
    sq = np.zeros((5, P, P), np.float32)
    sq[0] = np.eye(P)
    sq[1] = np.triu(np.ones((P, P)), 1)
    sq[2] = np.arange(P)
    sq[3, :, 0:16] = np.arange(16)
    tok = np.arange(NT)[None, :] * P + np.arange(P)[:, None]
    sq[3, :, 16:20] = tok + 1
    sq[3, :, 20:24] = 2 * tok + 1
    sq[3, :, 24:28] = np.arange(4)
    sq[3, :, 28:36] = np.arange(8)
    sq[3, :, 36] = EPS
    for r in range(HPG):
        a, m = divmod(r, 2)
        sq[4, r * 2 + m, a * HD:(a + 1) * HD] = 1.0
    tb = np.zeros((NBUCKET + 1, NG, GTW), np.float32)
    for g, dil in enumerate(DIL):
        for c in range(GTW):
            delta = 2 * P - 1 - c
            if g == 0:
                ok, dist = 0 <= delta <= P, delta
            elif g == 1:
                ok, dist = delta >= 0, delta * dil
            else:
                ok, dist = delta >= 0 and delta % 4 == 0, delta // 4 * dil
            if ok:
                tb[bucket(dist), g, c] = 1.0
            else:
                tb[NBUCKET, g, c] = NEG
    return sq, tb


_INS = ["x", "w_in", "w_attn_out", "w_conv_out", "w_o", "conv_w", "conv_b", "conv_ln_g", "conv_ln_b",
        "ln_mix_g", "ln_mix_b", "expert_w_gate_up", "expert_w_down", "ln_ffn_g", "ln_ffn_b", "router_w", "rel_bias"]


def kernel(**inputs):
    import concourse.bacc as bacc
    from concourse.bass_utils import run_bass_kernel_spmd

    nc = bacc.Bacc("TRN2", target_bir_lowering=False, num_devices=1)
    sq, tb = constants()
    arrays, args = {}, []
    for name, a in [(n, inputs[n]) for n in _INS] + [("c_square", sq), ("c_bucket", tb)]:
        a = np.ascontiguousarray(a)
        arrays[f"in_{name}"] = a
        args.append(nc.dram_tensor(f"in_{name}", a.shape, mybir.dt.from_np(a.dtype), kind="ExternalInput").ap())
    args.append(nc.dram_tensor("out_0", (1, S, D), F32, kind="ExternalOutput").ap())
    build(nc, *args)
    r = run_bass_kernel_spmd(nc, [arrays], core_ids=[0])
    return r.results[0]["out_0"]
```

```python
from contextlib import ExitStack
import math

import numpy as np

import concourse.bass as bass
from concourse import mybir

F32 = mybir.dt.float32
F32R = mybir.dt.float32r
I32 = mybir.dt.int32
ALU = mybir.AluOpType
ACT = mybir.ActivationFunctionType
AX = mybir.AxisListType

P = 128
D = 1024
S = 512
NT = S // P
KT = D // P
HD = 64
NG = 3
DIL = (1, 4, 16)
HPG = 4
GW = HPG * HD
AW = NG * GW
CW = D // 2
CT = CW // P
TAPS = 31
NBUCKET = 32
MAXDIST = 2048
NE = 16
EG = 4
FF = D
ALPHA = 2.0 ** 0.25
EPS = 1e-5
NEG = -1.0e30
GTW = 384

CH = 2048
CC = CH // KT
RM, HM = 3, 2
RE, HE = 12, 3
GU, DN = 8, 4
MAXBLK = 24
TAB = 32


def mixer_chunks():
    q0, k0, v0, u0, g0 = 0, AW, 2 * AW, 3 * AW, 3 * AW + 2 * CW
    out = []
    for half in range(2):
        out += [("in", u0 + half * CC), ("in", u0 + CW + half * CC)]
    for g in range(NG):
        out += [("in", q0 + g * GW), ("in", k0 + g * GW), ("in", v0 + g * GW)]
    out += [("in", g0 + D + c * CC) for c in range(4)]
    out += [("in", g0 + c * CC) for c in range(4)]
    out += [("conv", 0), ("conv", 1), ("attn", 0)]
    out += [("o", c) for c in range(4)]
    return out


CHUNKS = mixer_chunks()
NM = len(CHUNKS)

U_STEPS = range(0, 8)
QKV_STEPS = range(8, 26)
G1_STEPS = range(26, 34)
G0_STEPS = range(34, 42)
CONV_STEPS = range(42, 50)
ATTN_STEPS = range(50, 58)
UNITS = NG * NT
UNIT_STEP = [14 + u if u < 4 else 20 + u - 4 if u < 8 else 26 + u - 8 for u in range(UNITS)]
STEP_UNIT = {s: u for u, s in enumerate(UNIT_STEP)}


def chunk_of_step(s):
    if s < 42:
        return s // 2, s % 2 == 0, s % 2 == 1
    if s < 50:
        return 21 + (s - 42) // 4, (s - 42) % 4 == 0, (s - 42) % 4 == 3
    return 23, s == 50, s == 57


def conv_plan():
    quota = {s: 4 for s in range(4, 8)}
    quota.update({s: 6 for s in range(8, 14)})
    quota.update({s: 4 for s in range(14, 26)})
    quota.update({s: 4 for s in range(26, 34)})
    ops = [(j, k) for pair in range(2) for k in range(TAPS) for j in (2 * pair, 2 * pair + 1)]
    plan, at = {}, 0
    for s in range(4, 34):
        n = quota[s]
        if s < 8:
            n = min(n, 2 * TAPS - at)
        plan[s] = ops[at:at + n]
        at += len(plan[s])
    plan[33] = plan[33] + ops[at:]
    return plan


CONV_PLAN = conv_plan()
STEP_END = [s for s in range(58) if chunk_of_step(s)[2]]


def tokens(row, g, i):
    return row[..., i * P:(i + 1) * P] if g == 0 else row[..., i::4]


def build(nc, x, w_in, w_attn_out, w_conv_out, w_o, conv_w, conv_b, conv_ln_g, conv_ln_b,
          ln_mix_g, ln_mix_b, expert_w_gate_up, expert_w_down, ln_ffn_g, ln_ffn_b, router_w,
          rel_bias, c_square, c_bucket, out):
    ctx = ExitStack()
    with ctx:
        base = (nc.sbuf_base + 63) // 64 * 64
        KB = 1024

        def at(name, shape, dt, kb):
            return nc.alloc_sbuf_tensor_at(name, shape, dt, offset=base + int(kb * KB)).ap()

        def sem(name):
            return ctx.enter_context(nc.semaphore(name))

        xh = at("xh", [P, KT, S], F32R, 0)
        xl = at("xl", [P, KT, S], F32R, 16)
        raw_m = [at(f"raw_m{s}", [P, CH], F32, 32 + 8 * s) for s in range(RM)]
        hi_m = [at(f"hi_m{s}", [P, CH], F32R, 56 + 8 * s) for s in range(HM)]
        lo_m = [at(f"lo_m{s}", [P, CH], F32R, 72 + 8 * s) for s in range(HM)]
        qk = at("qk", [P, 2, 2, 2, S], F32, 88)
        sg0 = at("sg0", [P, KT, S], F32, 88)
        x1 = at("x1", [P, NT, D], F32, 88)
        vv = at("vv", [P, 2, NT, GW], F32, 104)
        bm = at("bm", [P, 2, 2, 2 * P], F32, 112)
        bm12 = at("bm12", [P, 2, 2, 2, P], F32, 116)
        sc = at("sc", [P, 2, 2, 2, 2 * P], F32, 120)
        glu = at("glu", [P, 2, S], F32, 120)
        aTh = at("aTh", [P, 2, S], F32R, 120)
        aTl = at("aTl", [P, 2, S], F32R, 124)
        pT = at("pT", [P, 2 * S], F32, 128)
        oT = at("oT", [P, NG, 2, S], F32, 132)
        sg1 = at("sg1", [P, KT, S], F32, 144)
        xt = at("xt", [P, NT, D], F32, 144)
        hg = at("hg", [P, CT, S + TAPS - 1], F32, 160)
        ctm = at("ctm", [P, NT, CW], F32, 160)
        cacc = at("cacc", [P, CT, S], F32, 168.5)
        ch = at("ch", [P, CT, S], F32R, 168.5)
        cl = at("cl", [P, CT, S], F32R, 176.5)
        cwt_rows = at("cwt_rows", [TAPS + 3, CW], F32, 132)
        btab = at("btab", [NBUCKET + 1, NG, GTW], F32, 176.5)
        gsb = at("gsb", [HPG, NG, GTW], F32, 181.5)
        lnm = at("lnm", [P, 2, D], F32, 186.5)
        csil = at("csil", [P, 2, S], F32, 128)
        RAW_KB = (32, 40, 48, 160, 176.5, 144, 152, 0, 8, 16, 24, 184.5)
        raw_e = raw_m + [at(f"raw_e{s}", [P, CH], F32, RAW_KB[s]) for s in range(RM, RE)]
        hi_e = hi_m + [at("hi_e2", [P, CH], F32R, 136)]
        lo_e = lo_m + [at("lo_e2", [P, CH], F32R, 168.5)]
        xe = at("xe", [P, D], F32, 104)
        xeh = at("xeh", [P, KT, P], F32R, 108)
        xel = at("xel", [P, KT, P], F32R, 112)
        he = at("he", [P, FF], F32, 116)
        heh = at("heh", [P, KT, P], F32R, 120)
        hel = at("hel", [P, KT, P], F32R, 124)
        pe_sel = at("pe_sel", [P, NT, P], F32, 128)
        ye = at("ye", [P, D], F32, 132)
        x1T = [at("x1T0", [P, D], F32, 128), at("x1T1", [P, D], F32, 132)]
        yt = [at(f"yt{t}", [P, 2, D], F32, RAW_KB[t]) for t in range(NT)]
        ot = [at(f"ot{t}", [P, D], F32, RAW_KB[4 + t // 2] + 4 * (t % 2)) for t in range(NT)]
        lnf = at("lnf", [P, 2, D], F32, RAW_KB[6])

        small = [194.5]

        def tiny(name, shape, dt=F32):
            n = int(np.prod(shape[1:])) * 4
            t = at(name, shape, dt, small[0])
            small[0] += (n + 31) // 32 * 32 / KB
            return t

        ident = tiny("ident", [P, P])
        upper = tiny("upper", [P, P])
        ones = tiny("ones", [P, P])
        iota = tiny("iota", [P, P])
        cwt = tiny("cwt", [P, CT, TAPS + 3])
        relb = tiny("relb", [NBUCKET + 1, NG * HPG])
        rw = tiny("rw", [P, KT, NE])
        cst = tiny("cst", [P, 64])
        nmx = tiny("nmx", [P, UNITS, HPG])
        den = tiny("den", [P, UNITS, HPG])
        rden = tiny("rden", [P, UNITS, HPG])
        lse = tiny("lse", [P, UNITS, HPG])
        stats = tiny("stats", [P, NT, 2, 6])
        mv = tiny("mv", [P, NT, 2])
        sd = tiny("sd", [P, NT, 1])
        nw = tiny("nw", [P, NT, 1])
        rstd = tiny("rstd", [P, NT, 1])
        spair = tiny("selpair", [HPG, 2, P])
        pr = tiny("pr", [P, NT, NE])
        t16a = tiny("t16a", [P, NT, NE])
        t16b = tiny("t16b", [P, NT, NE])
        s6 = tiny("s6", [P, NT * EG, 6])
        gsc = tiny("gsc", [P, NT, EG])
        gcd = tiny("gcd", [P, NT, EG])
        ohg = tiny("ohg", [P, NT, EG])
        oh1 = tiny("oh1", [P, NT, NE])
        oh2 = tiny("oh2", [P, NT, NE])
        sel = tiny("sel", [P, NT, NE])
        c4 = tiny("c4", [P, 8, NT])
        gwt = tiny("gwt", [P, 2, NT])
        vt = tiny("vt", [P, NE, NT, 3])
        cum = tiny("cum", [P, NT, NE])
        xtr = tiny("xtr", [P, NE])
        cs = tiny("cs", [P, 2, NE])
        ov = tiny("ov", [P, 8, NE])
        ov2 = tiny("ov2", [P, 8, NE])
        bbase = tiny("bbase", [P, TAB])
        etf = tiny("etf", [P, TAB])
        eti = tiny("eti", [P, TAB], I32)
        blk = tiny("blk", [P, NT, 3])
        idf = tiny("idf", [P, 2])
        idz = tiny("idz", [P, 2])
        gidx = tiny("gidx", [P, 1], I32)
        orow = tiny("orow", [P, MAXBLK], I32)
        sidx = tiny("sidx", [P, 1], I32)
        lsT = at("lsT", [HPG, NG, S], F32, 112)
        mxT = at("mxT", [HPG, S], F32, 118)
        assert base + small[0] * KB <= nc.sbuf_usable_end, small

        ps = ctx.enter_context(nc.psum_tensor("ps", [P, 8, S], F32)).ap()

        gtab = nc.dram_tensor("gtab", [NG * HPG, P, GTW], F32).ap()
        x1d = nc.dram_tensor("x1d", [S, D], F32).ap()
        yd = nc.dram_tensor("yd", [2 * S, D], F32).ap()

        raw_in = [sem(f"raw_in{s}") for s in range(RE)]
        hi_ready, lo_ready = sem("hi_ready"), sem("lo_ready")
        chunk_used = sem("chunk_used")
        x_in = [sem(f"x_in{t}") for t in range(NT)]
        sq_in, tab_in, cw_in, ln_in, small_in = (sem(n) for n in
                                                       ("sq_in", "tab_in", "cw_in", "ln_in", "small_in"))
        relb_one, pad_zero = sem("relb_one"), sem("pad_zero")
        cw_T, cw_ready = sem("cw_T"), sem("cw_ready")
        xT_done, xh_ready, xl_ready = sem("xT_done"), sem("xh_ready"), sem("xl_ready")
        gt_mm, gt_sb, gt_out, bm_in = sem("gt_mm"), sem("gt_sb"), sem("gt_out"), sem("bm_in")
        proj_done, proj_evac = sem("proj_done"), sem("proj_evac")
        glu_sig, glu_done = sem("glu_sig"), sem("glu_done")
        conv_op = sem("conv_op")
        att_s, s_add, s_max, att_exp, r_den, att_p = (sem(n) for n in
                                                      ("att_s", "s_add", "s_max", "att_exp", "r_den", "att_p"))
        att_t, pt_evac, att_o, o_evac = sem("att_t"), sem("pt_evac"), sem("att_o"), sem("o_evac")
        ln_den, lse_ready, lse_T, mixv, mix_exp, mix_F, mixc, aT_sum, aT_hi, aT_ready = (
            sem(n) for n in ("ln_den", "lse_ready", "lse_T", "mixv", "mix_exp", "mix_F", "mixc", "aT_sum", "aT_hi",
                             "aT_ready"))
        cT_done, cstat, cnorm, cb_T, c_silu, c_hi, c_ready = (
            sem(n) for n in ("cT_done", "cstat", "cnorm", "cb_T", "c_silu", "c_hi", "c_ready"))
        sig1, sig0 = sem("sig1"), sem("sig0")
        mcv, mga, merged_sum, m_hi, m_ready = (sem(n) for n in ("mcv", "mga", "merged_sum", "m_hi", "m_ready"))
        xr_in, wo_done, wo_used, lnv, x1_ready, x1_out = (
            sem(n) for n in ("xr_in", "wo_done", "wo_used", "lnv", "x1_ready", "x1_out"))
        x1_T, x1T_sb, logits, rv, r_exp, sel_ready, rank_mm, tables = (
            sem(n) for n in ("x1_T", "x1T_sb", "logits", "rv", "r_exp", "sel_ready", "rank_mm", "tables"))
        newton, residual = sem("newton"), sem("residual")
        ln1_scaled, x1_last = sem("ln1_scaled"), sem("x1_last")
        fin_w, fin_0, fin_last = sem("fin_w"), sem("fin_0"), sem("fin_last")
        gathers_begun, scatters_begun = sem("gathers_begun"), sem("scatters_begun")
        xe_zero, ones_set, lnf_in = sem("xe_zero"), sem("ones_set"), sem("lnf_in")
        bv, idv, sel_blk, idx_mm, idx_ready, xe_in, xe_T, xeh_ready, xel_ready = (
            sem(n) for n in ("bv", "idv", "sel_blk", "idx_mm", "idx_ready", "xe_in", "xe_T", "xeh_ready", "xel_ready"))
        silu_done, he_ready, he_T, heh_ready, hel_ready, ye_ready, y_out = (
            sem(n) for n in ("silu_done", "he_ready", "he_T", "heh_ready", "hel_ready",
                             "ye_ready", "y_out"))
        sidx_ready = sem("sidx_ready")
        yt_in = [sem(f"yt_in{t}") for t in range(NT)]
        fin_s, fin_a, fv, fin_ready, gv, lgv, crstd, lrstd, frstd, csd, lsd, fsd = (
            sem(n) for n in ("fin_s", "fin_a", "fv", "fin_ready", "gv", "lgv", "crstd", "lrstd", "frstd", "csd", "lsd", "fsd"))
        out_st = sem("out_st")

        win_v = w_in.rearrange("a (k p) c -> p (a k) c", p=P)
        wco_v = w_conv_out.rearrange("a (k p) c -> p (a k) c", p=P)
        wao_v = w_attn_out.rearrange("a (k p) c -> p (a k) c", p=P)
        wo_v = w_o.rearrange("a (k p) c -> p (a k) c", p=P)
        wgu_v = expert_w_gate_up.rearrange("a e (k p) c -> (a e) k p c", p=P)
        wdn_v = expert_w_down.rearrange("a e (c k p) n -> (a e) c p k n", p=P, k=2)
        x_v = x.rearrange("b (t p) d -> p (b t) d", p=P)
        out_v = out.rearrange("b (t p) d -> (b t) p d", p=P)
        x1d_v = x1d.rearrange("(t p) d -> t p d", p=P)
        yd_v = yd.rearrange("(t p k) d -> t p k d", p=P, k=2)

        def mixer_source(n):
            kind, c = CHUNKS[n]
            if kind == "in":
                return win_v[:, :, c:c + CC]
            if kind == "conv":
                return wco_v[:, :, c * 512:(c + 1) * 512]
            if kind == "attn":
                return wao_v
            return wo_v[:, 2 * c:2 * c + 2, :]

        def in_tiles(tile, n):
            kind, _ = CHUNKS[n]
            k = {"in": KT, "conv": CT, "attn": 2, "o": 2}[kind]
            return tile.rearrange("p (k c) -> p k c", k=k)

        M_USES = [len(range(s, NM, RM)) for s in range(RM)] + [0] * (RE - RM)

        def landed(b, q):
            return b * 16 + 16 * (M_USES[q % RE] + q // RE + 1)

        block = ctx.enter_context(nc.Block())

        @block.sync
        def _(sp):
            def fetch(q, src):
                dst = raw_e[q % RE]
                if len(src.shape) == 3:
                    dst = dst.rearrange("p (k c) -> p k c", k=2)
                sp.dma_start(dst, src).then_inc(raw_in[q % RE], 16)

            def load(b, q, src):
                sp.wait_ge(lo_ready, b * 12 + (NM + q - RE + 1))
                fetch(q, src)

            def block_chunks(b, cur, prev):
                for c in range(GU):
                    load(b, GU + c, expert(wgu_v, cur)[c])
                for c in range(DN):
                    load(b, 2 * GU + c, expert(wdn_v, prev)[c])

            def expert(v, e):
                return v[e] if isinstance(e, int) else v[bass.ds(e, 1)].rearrange(
                    "a c p n -> (a c) p n" if len(v.shape) == 4 else "a c p k n -> (a c) p k n")

            for t in range(NT):
                sp.dma_start(xt[:, t], x_v[:, t]).then_inc(x_in[t], 16)
            for n in range(NM):
                if n >= RM:
                    sp.wait_ge(lo_ready, n - RM + 1)
                if n == 23:
                    sp.wait_ge(cb_T, CT)
                    fetch(3, wgu_v[0, 3])
                elif n == NM - 1:
                    sp.wait_ge(proj_done, 50)
                    fetch(4, wgu_v[0, 4])
                sp.dma_start(in_tiles(raw_m[n % RM], n), mixer_source(n)).then_inc(raw_in[n % RM], 16)
            for c in (1, 2, 5, 6, 0, 7):
                if c < RM:
                    last = max(n for n in range(NM) if n % RM == c)
                    sp.wait_ge(lo_ready, last + 1)
                elif c == 5:
                    sp.wait_ge(m_ready, KT)
                elif c == 7:
                    sp.wait_ge(wo_done, NT)
                fetch(c, wgu_v[0, c])
            for c in range(GU):
                if GU + c == RE - 1:
                    sp.wait_ge(x1_ready, NT - 1)
                    sp.wait_ge(x1_last, 1)
                if GU + c < RE:
                    fetch(GU + c, wgu_v[1, c])
                else:
                    load(0, GU + c, wgu_v[1, c])
            for c in range(DN):
                load(0, 2 * GU + c, wdn_v[0, c])

            with sp.Fori(2, NE) as i:
                block_chunks(i - 1, i, i - 1)
            sp.wait_ge(tables, 1)
            nblk = sp.value_load(eti[0:1, TAB - 1:TAB], min_val=0, max_val=MAXBLK - 1 - NE) + NE
            with sp.If(nblk > NE):
                with sp.Fori(NE, nblk) as i:
                    cur = sp.value_load(eti[0:1, bass.ds(i, 1)], min_val=0, max_val=NE - 1)
                    prev = sp.value_load(eti[0:1, bass.ds(i - 1, 1)], min_val=0, max_val=NE - 1)
                    block_chunks(i - 1, cur, prev)
            final = sp.value_load(eti[0:1, bass.ds(nblk - 1, 1)], min_val=0, max_val=NE - 1)
            for c in range(DN):
                load(nblk - 1, GU + c, expert(wdn_v, final)[c])
            sp.wait_ge(lo_ready, nblk * 12 + (NM - RE + 6 + 1))
            for j, v in enumerate((ln_ffn_g, ln_ffn_b)):
                sp.dma_start(lnf[:, j], bass.AP(v.tensor, 0, [[0, P], [1, D]])).then_inc(lnf_in, 16)
            sp.wait_ge(y_out, nblk * 16)
            for t in range(NT):
                sp.dma_start(yt[t], yd_v[t]).then_inc(yt_in[t], 16)
            for t in range(NT):
                if t < NT - 1:
                    sp.wait_ge(fin_ready, t + 1)
                else:
                    sp.wait_ge(fin_last, 1)
                sp.dma_start(out_v[t], ot[t]).then_inc(out_st, 16)
            sp.wait_ge(out_st, 16 * NT)

        @block.gpsimd
        def _(pool):
            pool.memset(ones, 1.0).then_inc(ones_set, 1)
            pool.dma_start(ident, c_square[0]).then_inc(sq_in, 16)
            pool.dma_start(cwt_rows[0:TAPS], conv_w[0]).then_inc(cw_in, 16)
            pool.dma_start(cwt_rows[TAPS:TAPS + 1], conv_b).then_inc(cw_in, 16)
            pool.dma_start(cwt_rows[TAPS + 1:TAPS + 2], conv_ln_g).then_inc(cw_in, 16)
            pool.dma_start(cwt_rows[TAPS + 2:TAPS + 3], conv_ln_b).then_inc(cw_in, 16)
            pool.dma_start(btab, c_bucket).then_inc(tab_in, 16)
            pool.dma_start(relb[0:NBUCKET], rel_bias).then_inc(tab_in, 16)
            pool.dma_start(upper, c_square[1]).then_inc(small_in, 16)
            pool.dma_start(iota, c_square[2]).then_inc(small_in, 16)
            pool.dma_start(cst, c_square[3, :, 0:64]).then_inc(small_in, 16)
            pool.dma_start(spair, c_square[4, 0:2 * HPG, :].rearrange("(h m) c -> h m c", m=2)).then_inc(small_in, 16)
            pool.dma_start(rw, router_w.rearrange("(k p) e -> p k e", p=P)).then_inc(small_in, 16)
            for j, v in enumerate((ln_mix_g, ln_mix_b)):
                pool.dma_start(lnm[:, j], bass.AP(v.tensor, 0, [[0, P], [1, D]])).then_inc(ln_in, 16)
            pool.wait_ge(gt_sb, NG)
            for g in range(NG):
                pool.dma_start(gtab[g * HPG:(g + 1) * HPG], bass.AP(gsb.tensor, gsb[:, g].offset,
                               [list(gsb.ap[0]), [0, P], [1, GTW]])).then_inc(gt_out, 16)
            pool.wait_ge(gt_out, 16 * NG)
            for a in range(2):
                pool.dma_start(bm[:, a], bass.AP(gtab.tensor, a * P * GTW + P - 1,
                                                     [[GTW - 1, P], [2 * P * GTW, 2], [1, 2 * P]])
                               ).then_inc(bm_in, 16)
                for g in (1, 2):
                    pool.dma_start(bm12[:, g - 1, a], bass.AP(gtab.tensor, (HPG * g + a) * P * GTW + 2 * P - 1,
                                                             [[GTW - 1, P], [2 * P * GTW, 2], [1, P]])).then_inc(bm_in, 16)
            pool.wait_ge(ln_in, 32)
            pool.wait_ge(m_ready, KT)
            pool.dma_start(x1, x_v).then_inc(xr_in, 16)
            for t in range(NT):
                if t < NT - 1:
                    pool.wait_ge(ln1_scaled, t + 1)
                    pool.tensor_tensor(x1[:, t], x1[:, t], lnm[:, 1], ALU.add).then_inc(x1_ready, 1)
                    pool.wait_ge(x1_ready, t + 1)
                else:
                    pool.wait_ge(x1_last, 1)
                pool.dma_start(x1d_v[t], x1[:, t]).then_inc(x1_out, 16)
            pool.wait_ge(x1_out, 16 * NT)
            pool.memset(xe, 0.0).then_inc(xe_zero, 1)

            def gather(i):
                pool.wait_ge(idx_ready, i + 1)
                pool.sem_inc(gathers_begun, 1)
                pool.indirect_dma_start(xe, None, x1d, bass.IndirectOffsetOnAxis(gidx[:, 0:1], 0),
                                        bounds_check=S - 1, oob_is_err=False).then_inc(xe_in, 16)

            def scatter(i):
                pool.wait_ge(sidx_ready, i + 1)
                pool.wait_ge(ye_ready, i + 1)
                pool.sem_inc(scatters_begun, 1)
                pool.indirect_dma_start(yd, bass.IndirectOffsetOnAxis(sidx[:, 0:1], 0), ye, None,
                                        bounds_check=2 * S - 1, oob_is_err=False).then_inc(y_out, 16)

            pool.wait_ge(xe_zero, 1)
            gather(0)
            for i in range(2):
                pool.wait_ge(xe_T, i + 1)
                gather(i + 1)
            scatter(0)
            pool.wait_ge(xe_T, 3)
            gather(3)
            pool.wait_ge(tables, 1)
            nblk = pool.value_load(eti[0:1, TAB - 1:TAB], min_val=0, max_val=MAXBLK - 1 - NE) + NE
            with pool.Fori(3, nblk) as i:
                scatter(i - 2)
                pool.wait_ge(xe_T, i + 1)
                gather(i + 1)
            for k in (2, 1):
                scatter(nblk - k)
            pool.wait_ge(residual, 1)
            pool.wait_ge(lnf_in, 32)
            for t in range(1, NT + 1):
                if t < NT:
                    pool.wait_ge(fin_w, t)
                    pool.tensor_tensor(ot[t], yt[t][:, 0], x1[:, t], ALU.add).then_inc(fin_a, 1)
                if t >= 2:
                    pool.wait_ge(fin_s, t - 1)
                    pool.tensor_tensor(ot[t - 2], ot[t - 2], lnf[:, 1], ALU.add).then_inc(fin_ready, 1)

        @block.tensor
        def _(pe):
            def three(dst, a, b, c, d, first, last):
                pe.matmul(dst, a, c, start=first, stop=False)
                pe.matmul(dst, a, d, start=False, stop=False)
                return pe.matmul(dst, b, c, start=False, stop=last)

            pe.wait_ge(sq_in, 16)
            for t in range(NT):
                pe.wait_ge(x_in[t], 16)
                for k in range(KT):
                    mm = pe.transpose(ps[:, k, t * P:(t + 1) * P], xt[:, t, k * P:(k + 1) * P], ident)
                    if t == NT - 1:
                        mm.then_inc(xT_done, 1)
            def scores(u):
                g, i = divmod(u, NT)
                w = 2 * P if g == 0 and i > 0 else P
                pe.wait_ge(proj_evac, 6 * g + 4)
                if u >= 1:
                    pe.wait_ge(s_add, u)
                if u == 0:
                    pe.wait_ge(glu_done, CT)
                for a in range(2):
                    for m in range(2):
                        q = qk[a * HD:(a + 1) * HD, g % 2, 0, m]
                        k = qk[a * HD:(a + 1) * HD, g % 2, 1, m]
                        keys = k[:, (i - 1) * P:(i + 1) * P] if w > P else tokens(k, g, i)
                        mm = pe.matmul(ps[:, 2 + a, m * w:(m + 1) * w], tokens(q, g, i), keys, start=True, stop=True)
                mm.then_inc(att_s, 1)

            def transpose_probs(u):
                g, i = divmod(u, NT)
                w = 2 * P if g == 0 and i > 0 else P
                pe.wait_ge(att_p, u + 1)
                if u >= 1:
                    pe.wait_ge(pt_evac, u)
                for kt in range(w // P):
                    for a in range(2):
                        for m in range(2):
                            mm = pe.transpose(ps[:, 4 + kt, (2 * a + m) * P:(2 * a + m + 1) * P],
                                              sc[:, u % 2, a, m, kt * P:(kt + 1) * P], ident)
                mm.then_inc(att_t, 1)

            def weighted_values(u):
                g, i = divmod(u, NT)
                tiles = [i - 1, i] if g == 0 and i > 0 else [i]
                pe.wait_ge(pt_evac, u + 1)
                pe.wait_ge(proj_evac, 6 * g + 6)
                if u >= 1:
                    pe.wait_ge(o_evac, u)
                for a in range(2):
                    for m in range(2):
                        h = 2 * m + a
                        for n, kt in enumerate(tiles):
                            mm = pe.matmul(ps[a * HD:(a + 1) * HD, 6, m * P:(m + 1) * P],
                                           vv[:, g % 2, kt, h * HD:(h + 1) * HD],
                                           pT[:, n * S + (2 * a + m) * P:n * S + (2 * a + m + 1) * P],
                                           start=(n == 0), stop=(n == len(tiles) - 1))
                mm.then_inc(att_o, 1)

            for s in range(58):
                if s == 2:
                    pe.wait_ge(cw_in, 64)
                    pe.wait_ge(xl_ready, 5)
                    for j in range(CT):
                        mm = pe.transpose(ps[:, 4, j * 64:j * 64 + TAPS + 3], cwt_rows[:, j * P:(j + 1) * P],
                                          ident[0:TAPS + 3, 0:TAPS + 3])
                    mm.then_inc(cw_T, 1)
                    pe.wait_ge(tab_in, 32)
                    pe.wait_ge(relb_one, 1)
                    for g in range(NG):
                        pe.wait_ge(xl_ready, 6 + g)
                        pe.matmul(ps[0:HPG, 5 + g, 0:GTW],
                                  relb[:, HPG * g:HPG * (g + 1)],
                                  btab[:, g], start=True, stop=True).then_inc(gt_mm, 1)
                if s in STEP_UNIT:
                    scores(STEP_UNIT[s])
                if s - 1 in STEP_UNIT:
                    transpose_probs(STEP_UNIT[s - 1])
                if s - 2 in STEP_UNIT:
                    weighted_values(STEP_UNIT[s - 2])
                if s == 33:
                    pe.wait_ge(lse_ready, 1)
                    pe.wait_ge(pt_evac, UNITS)
                    for u in range(UNITS):
                        g, i = divmod(u, NT)
                        mm = pe.transpose(ps[0:HPG, 2 + g, i * P:(i + 1) * P], lse[:, u], ident)
                    mm.then_inc(lse_T, 1)
                if s == 35:
                    pe.wait_ge(conv_op, CT * TAPS)
                    pe.wait_ge(mixv, 3)
                    pe.wait_ge(o_evac, UNITS)
                    for t in range(NT):
                        for j in range(CT):
                            mm = pe.transpose(ps[:, 4 + t, j * P:(j + 1) * P], cacc[:, j, t * P:(t + 1) * P], ident)
                        mm.then_inc(cT_done, 1)
                if s == 39:
                    pe.wait_ge(cnorm, NT)
                    for j in range(CT):
                        for t in range(NT):
                            mm = pe.transpose(ps[:, 4 + j, t * P:(t + 1) * P], ctm[:, t, j * P:(j + 1) * P], ident)
                        mm.then_inc(cb_T, 1)
                if s == 41:
                    pe.wait_ge(mixv, 10)
                    pe.wait_ge(c_silu, CT)
                    for m in range(2):
                        for g in range(NG):
                            pe.matmul(ps[:, 2 + NG * m + g], spair[:, m], lsT[:, g], start=True, stop=True
                                      ).then_inc(mix_F, 1)
                n, first, last = chunk_of_step(s)
                if first:
                    pe.wait_ge(lo_ready, n + 1)
                h_, l_ = in_tiles(hi_m[n % HM], n), in_tiles(lo_m[n % HM], n)
                if s < 8:
                    bank = s
                    if s == 4:
                        pe.wait_ge(cw_ready, 1)
                    if 5 <= s:
                        pe.wait_ge(gt_sb, s - 4)
                else:
                    bank = s % 2
                    if s < 10:
                        pe.wait_ge(glu_done, s - 7)
                    elif s < 43:
                        pe.wait_ge(proj_evac, s - 9)
                    elif s < 44:
                        pe.wait_ge(proj_evac, 34)
                    elif s < 52:
                        pe.wait_ge(mcv, s - 43)
                    elif s == 52:
                        pe.wait_ge(mixc, 8)
                    if s >= 50:
                        bank = s - 50
                if s in QKV_STEPS and (s - 8) % 6 >= 4:
                    g, half = (s - 8) // 6, (s - 8) % 6 - 4
                    for q in range(2):
                        i = 2 * half + q
                        for k in range(KT):
                            mm = three(ps[:, bank, q * GW:(q + 1) * GW], tokens(xh[:, k], g, i), tokens(xl[:, k], g, i),
                                       h_[:, k], l_[:, k], k == 0, k == KT - 1)
                elif s < 42:
                    cols = slice((s % 2) * P, (s % 2 + 1) * P)
                    for k in range(KT):
                        if s == 0:
                            pe.wait_ge(xl_ready, k + 1)
                        mm = three(ps[:, bank], h_[:, k, cols], l_[:, k, cols], xh[:, k], xl[:, k],
                                   k == 0, k == KT - 1)
                elif s < 50:
                    if s == 42:
                        pe.wait_ge(c_ready, CT)
                    cols = slice((s - 42) % 4 * P, ((s - 42) % 4 + 1) * P)
                    for k in range(CT):
                        mm = three(ps[:, bank], h_[:, k, cols], l_[:, k, cols], ch[:, k], cl[:, k],
                                   k == 0, k == CT - 1)
                else:
                    if s == 50:
                        pe.wait_ge(aT_ready, 2)
                    cols = slice((s - 50) * P, (s - 49) * P)
                    for k in range(2):
                        mm = three(ps[:, bank], h_[:, k, cols], l_[:, k, cols], aTh[:, k], aTl[:, k],
                                   k == 0, k == 1)
                mm.then_inc(proj_done, 1)
            def transpose_x1(t):
                if t < NT - 1:
                    pe.wait_ge(x1_ready, t + 1)
                else:
                    pe.wait_ge(x1_last, 1)
                for k in range(KT):
                    mm = pe.transpose(ps[:, 2 * t + k // 4, k % 4 * P:(k % 4 + 1) * P],
                                      x1[:, t, k * P:(k + 1) * P], ident)
                mm.then_inc(x1_T, 1)

            order = [(c, t) for c in range(2) for t in range(NT)]
            order += [(2, 0), (2, 1), (3, 0), (3, 1), (2, 2), (3, 2), (2, 3), (3, 3)]
            for place, (c, t) in enumerate(order):
                n = 24 + c
                h_, l_ = in_tiles(hi_m[n % HM], n), in_tiles(lo_m[n % HM], n)
                if c not in [o[0] for o in order[:place]]:
                    pe.wait_ge(lo_ready, n + 1)
                    pe.wait_ge(m_ready, 2 * c + 2)
                if (c, t) == order[-1]:
                    transpose_x1(0)
                tok = slice(t * P, (t + 1) * P)
                for half in range(2):
                    if c == 0:
                        pe.wait_ge(mga, 2 * t + half + 1)
                    for k in range(2):
                        kk = 2 * c + k
                        col = slice(half * 512, (half + 1) * 512)
                        mm = three(ps[:, 2 * t + half], xh[:, kk, tok], xl[:, kk, tok], h_[:, k, col],
                                   l_[:, k, col], kk == 0, kk == KT - 1)
                if c == 3:
                    mm.then_inc(wo_done, 1)
                elif t == NT - 1:
                    mm.then_inc(wo_used, 1)
            pe.wait_ge(small_in, 80)
            def router_logits(t):
                pe.wait_ge(x1T_sb, t + 1)
                for k in range(KT):
                    mm = pe.matmul(ps[:, 2 * t, 0:NE], x1T[t % 2][:, k * P:(k + 1) * P], rw[:, k],
                                   start=(k == 0), stop=(k == KT - 1))
                mm.then_inc(logits, 1)

            transpose_x1(1)
            router_logits(0)
            router_logits(1)
            transpose_x1(2)
            transpose_x1(3)
            router_logits(2)
            router_logits(3)
            pe.wait_ge(sel_ready, 1)
            pe.wait_ge(ones_set, 1)
            selv = sel.rearrange("p t e -> p (t e)")
            pe.matmul(ps[:, 1, 0:NT * NE], upper, selv, start=True, stop=True)
            pe.matmul(ps[:, 3, 0:NT * NE], ones, selv, start=True, stop=True).then_inc(rank_mm, 1)

            def lookup(i):
                pe.wait_ge(sel_blk, i + 1)
                for t in range(NT):
                    mm = pe.matmul(ps[:, 4, 0:2], pe_sel[:, t], blk[:, t, 0:2], start=(t == 0), stop=(t == NT - 1))
                mm.then_inc(idx_mm, 1)

            def transpose_rows(i):
                if not (isinstance(i, int) and i < 2):
                    pe.wait_ge(heh_ready, i - 1)
                    pe.wait_ge(hel_ready, i - 1)
                pe.wait_ge(xe_in, 16 * i + 16)
                for k in range(KT):
                    mm = pe.transpose(ps[:, 6 + k // 4, k % 4 * P:(k % 4 + 1) * P], xe[:, k * P:(k + 1) * P], ident)
                mm.then_inc(xe_T, 1)

            def gate_up(i, b, q0):
                pe.wait_ge(xel_ready, i + 1)
                pe.wait_ge(xeh_ready, i + 1)
                if q0:
                    pe.wait_ge(he_ready, i)
                for c in range(GU):
                    q = q0 + c
                    h_, l_ = hi_e[q % HE], lo_e[q % HE]
                    pe.wait_ge(lo_ready, b * 12 + (NM + q + 1))
                    for n, (rows, cols) in enumerate(((xeh, h_), (xeh, l_), (xel, h_))):
                        for k in range(4):
                            mm = pe.matmul(ps[:, k], rows[:, c], cols[:, k * 512:(k + 1) * 512],
                                           start=(c == 0 and n == 0), stop=(c == GU - 1 and n == 2))
                    mm.then_inc(chunk_used, 1)
                    if c == 0:
                        if not (isinstance(i, int) and i < 2):
                            pe.wait_ge(ye_ready, i - 1)
                        lookup(i + 1)
                transpose_rows(i + 1)

            def down(i, b, q0, prev, last=False):
                pe.wait_ge(heh_ready, i + 1)
                pe.wait_ge(hel_ready, i + 1)
                if prev:
                    pe.wait_ge(ye_ready, i)
                if not last:
                    pe.wait_ge(idx_ready, i + 3)
                for c in range(DN):
                    q = q0 + c
                    h_, l_ = hi_e[q % HE], lo_e[q % HE]
                    pe.wait_ge(lo_ready, b * 12 + (NM + q + 1))
                    for k in range(2):
                        for n, (rows, cols) in enumerate(((heh, h_), (heh, l_), (hel, h_))):
                            for half in range(2):
                                mm = pe.matmul(ps[:, 4 + half], rows[:, 2 * c + k],
                                               cols[:, k * D + half * 512:k * D + (half + 1) * 512],
                                               start=(c + k + n == 0), stop=(c == DN - 1 and k == 1 and n == 2))
                    mm.then_inc(chunk_used, 1)

            def transpose_hidden(i):
                pe.wait_ge(he_ready, i + 1)
                pe.wait_ge(xel_ready, i + 2)
                pe.wait_ge(xeh_ready, i + 2)
                for k in range(KT):
                    mm = pe.transpose(ps[:, 6 + k // 4, k % 4 * P:(k % 4 + 1) * P], he[:, k * P:(k + 1) * P], ident)
                mm.then_inc(he_T, 1)

            lookup(0)
            transpose_rows(0)
            gate_up(0, 0, 0)
            transpose_hidden(0)
            gate_up(1, 0, GU)
            down(0, 0, 2 * GU, False)
            transpose_hidden(1)
            gate_up(2, 1, GU)
            down(1, 1, 2 * GU, True)
            transpose_hidden(2)
            pe.wait_ge(tables, 1)
            nblk = pe.value_load(eti[0:1, TAB - 1:TAB], min_val=0, max_val=MAXBLK - 1 - NE) + NE
            with pe.Fori(3, nblk) as i:
                gate_up(i, i - 1, GU)
                down(i - 1, i - 1, 2 * GU, True)
                transpose_hidden(i)
            down(nblk - 1, nblk - 1, GU, True, last=True)

        @block.scalar
        def _(act):
            def cut(n):
                act.wait_ge(raw_in[n % RM], 16 * (n // RM + 1))
                if HM <= n < 24 + HM:
                    act.wait_ge(proj_done, STEP_END[n - HM] + 1)
                elif n >= HM:
                    act.wait_ge(wo_used, n - HM - 23)
                act.activation(hi_m[n % HM], raw_m[n % RM], ACT.Copy).then_inc(hi_ready, 1)

            def deviation(t, wait, n, done):
                act.wait_ge(wait, n)
                act.activation(sd[:, t], mv[:, t, 1:2], ACT.Sqrt, bias=cst[:, 36:37]).then_inc(done, 1)

            for k in range(KT):
                act.wait_ge(xT_done, k + 1)
                act.activation(xh[:, k], ps[:, k], ACT.Copy).then_inc(xh_ready, 1)
                if k == 4:
                    cut(0)

            def evacuate(s):
                act.wait_ge(proj_done, s + 1)
                if s in U_STEPS:
                    if s % 4 >= 2:
                        c = s // 4 * 2 + s % 4 - 2
                        if c >= 2:
                            act.wait_ge(glu_done, c - 1)
                        act.activation(glu[:, c % 2], ps[:, s], ACT.Sigmoid).then_inc(glu_sig, 1)
                elif s in QKV_STEPS:
                    g, r = divmod(s - 8, 6)
                    if g == 2 and r == 0:
                        act.wait_ge(att_s, NT)
                    if g == 2 and r == 4:
                        act.wait_ge(att_o, NT)
                    if r < 4:
                        act.activation(qk[:, g % 2, r // 2, r % 2], ps[:, s % 2], ACT.Copy,
                                       scale=HD ** -0.5 if r < 2 else 1.0).then_inc(proj_evac, 1)
                    else:
                        act.activation(vv[:, g % 2, 2 * (r - 4):2 * (r - 4) + 2],
                                       ps[:, s % 2].rearrange("p (i c) -> p i c", i=2), ACT.Copy).then_inc(proj_evac, 1)
                elif s in G1_STEPS:
                    act.activation(sg1[:, s - 26], ps[:, s % 2], ACT.Copy).then_inc(proj_evac, 1)
                elif s in G0_STEPS:
                    if s == 34:
                        act.wait_ge(att_s, UNITS)
                    act.activation(sg0[:, s - 34], ps[:, s % 2], ACT.Copy).then_inc(proj_evac, 1)

            def exponentials(u):
                g, i = divmod(u, NT)
                w = 2 * P if g == 0 and i > 0 else P
                act.wait_ge(s_max, u + 1)
                for a in range(2):
                    for m in range(2):
                        h = 2 * a + m
                        e = act.activation(sc[:, u % 2, a, m, 0:w], sc[:, u % 2, a, m, 0:w], ACT.Exp,
                                           bias=nmx[:, u, h:h + 1], accum_out=den[:, u, h:h + 1])
                e.then_inc(att_exp, 1)

            def probs_T(u):
                g, i = divmod(u, NT)
                w = 2 if g == 0 and i > 0 else 1
                act.wait_ge(att_t, u + 1)
                if u >= 1:
                    act.wait_ge(att_o, u)
                act.activation(pT[:, 0:w * S], ps[:, 4:4 + w].rearrange("p a c -> p (a c)"), ACT.Copy).then_inc(pt_evac, 1)

            def outputs_T(u):
                g, i = divmod(u, NT)
                act.wait_ge(att_o, u + 1)
                if u == 0:
                    act.wait_ge(cw_ready, 1)
                src = ps[:, 6, 0:2 * P].rearrange("p (m c) -> p m c", m=2)
                act.activation(tokens(oT[:, g], g, i), src, ACT.Copy).then_inc(o_evac, 1)

            for s in range(58):
                n, first, last = chunk_of_step(s)
                if 1 <= s <= 42:
                    evacuate(s - 1)
                if s - 1 in STEP_UNIT:
                    probs_T(STEP_UNIT[s - 1])
                if s - 2 in STEP_UNIT:
                    outputs_T(STEP_UNIT[s - 2])
                if s in STEP_UNIT:
                    exponentials(STEP_UNIT[s])
                if first and n + 1 <= 24:
                    cut(n + 1)
                if s == 1:
                    act.wait_ge(cw_T, 1)
                    act.activation(cwt, ps[:, 4, 0:64 * CT].rearrange("p (j k) -> p j k", k=64)[:, :, 0:TAPS + 3],
                                   ACT.Copy).then_inc(cw_ready, 1)
                    for g in range(NG):
                        act.wait_ge(gt_mm, g + 1)
                        act.activation(gsb[:, g], ps[0:HPG, 5 + g, 0:GTW], ACT.Copy).then_inc(gt_sb, 1)
                if s == 31:
                    act.wait_ge(r_den, UNITS)
                    act.activation(lse, den, ACT.Ln).then_inc(ln_den, 1)
                if s == 37:
                    act.wait_ge(mixv, 6)
                    act.activation(lsT, lsT, ACT.Exp).then_inc(mix_exp, 1)
                if s == 35:
                    act.wait_ge(small_in, 80)
                    for t in range(NT):
                        deviation(t, cstat, 2 * t + 2, csd)
                if s == 39:
                    for j in range(CT):
                        act.wait_ge(cb_T, j + 1)
                        if j >= 2:
                            act.wait_ge(c_ready, j - 1)
                        act.activation(csil[:, j % 2], ps[:, 4 + j], ACT.Silu, scale=cwt[:, j, TAPS + 1:TAPS + 2],
                                       bias=cwt[:, j, TAPS + 2:TAPS + 3]).then_inc(c_silu, 1)
                        act.wait_ge(c_silu, j + 1)
                        act.activation(ch[:, j], csil[:, j % 2], ACT.Copy).then_inc(c_hi, 1)
                if s == 41:
                    act.wait_ge(proj_evac, 26)
                    act.activation(sg1, sg1, ACT.Sigmoid).then_inc(sig1, 1)
                if s == 42:
                    for m in range(2):
                        act.wait_ge(aT_sum, m + 1)
                        act.activation(aTh[:, m], oT[:, 0, m], ACT.Copy).then_inc(aT_hi, 1)
                if s == 42:
                    act.wait_ge(proj_evac, 34)
                    act.activation(sg0, sg0, ACT.Sigmoid).then_inc(sig0, 1)
                if s >= 51:
                    act.wait_ge(merged_sum, s - 50)
                    act.activation(xh[:, s - 51], sg1[:, s - 51], ACT.Copy).then_inc(m_hi, 1)
                if s == 57:
                    cut(25)
            act.wait_ge(merged_sum, KT)
            act.activation(xh[:, KT - 1], sg1[:, KT - 1], ACT.Copy).then_inc(m_hi, 1)
            for n in range(26, NM):
                cut(n)

            def cut_e(b, q):
                act.wait_ge(raw_in[q % RE], landed(b, q))
                if q >= HE:
                    act.wait_ge(chunk_used, b * 12 + (q - HE + 1))
                act.activation(hi_e[q % HE], raw_e[q % RE], ACT.Copy).then_inc(hi_ready, 1)

            for t in range(NT + 1):
                if t < NT:
                    deviation(t, lnv, 4 * t + 4, lsd)
                if t < NT - 1:
                    act.wait_ge(lrstd, 3 * t + 3)
                    act.wait_ge(gv, t + 1)
                    act.activation(x1[:, t], x1[:, t], ACT.Copy, scale=rstd[:, t]).then_inc(ln1_scaled, 1)
                if t >= 1:
                    act.wait_ge(x1_T, t)
                    if t >= 3:
                        act.wait_ge(logits, t - 2)
                    act.activation(x1T[(t - 1) % 2], ps[:, 2 * t - 2:2 * t].rearrange("p a c -> p (a c)"), ACT.Copy
                                   ).then_inc(x1T_sb, 1)
                if t == 3:
                    cut_e(0, 0)
            act.wait_ge(rv, 2)
            act.activation(pr, pr, ACT.Exp).then_inc(r_exp, 1)
            for m in range(1, HE):
                cut_e(0, m)

            def two_banks(bank):
                return ps[:, bank:bank + 2].rearrange("p a c -> p (a c)")

            def rows_hi(i):
                act.wait_ge(xe_T, i + 1)
                act.activation(xeh.rearrange("p k c -> p (k c)"), two_banks(6), ACT.Copy).then_inc(xeh_ready, 1)

            def hidden_hi(i):
                act.wait_ge(he_T, i + 1)
                act.activation(heh.rearrange("p k c -> p (k c)"), two_banks(6), ACT.Copy).then_inc(heh_ready, 1)

            def output(i, b, q):
                act.wait_ge(chunk_used, b * 12 + (q + 1))
                if not (isinstance(i, int) and i == 0):
                    act.wait_ge(y_out, i * 16)
                act.activation(ye, two_banks(4), ACT.Copy).then_inc(ye_ready, 1)

            def body(i, b, q0, n_chunks, skip=0, prev=True, prev2=True):
                for c in range(skip, n_chunks):
                    cut_e(b, q0 + c)
                    if c == 2 and prev2:
                        output(i - 2, b, q0 - 1)
                    if c == (2 if n_chunks > DN else 0) and prev:
                        hidden_hi(i - 1)
                    if c == min(GU + 2, n_chunks - 1) and n_chunks > DN:
                        act.wait_ge(chunk_used, b * 12 + (q0 + GU))
                        act.activation(he, two_banks(0), ACT.Silu).then_inc(silu_done, 1)
                        rows_hi(i + 1)

            rows_hi(0)
            body(0, 0, 0, GU, skip=HE, prev=False, prev2=False)
            body(1, 0, GU, GU + DN, prev2=False)
            body(2, 1, GU, GU + DN)
            act.wait_ge(tables, 1)
            nblk = act.value_load(eti[0:1, TAB - 1:TAB], min_val=0, max_val=MAXBLK - 1 - NE) + NE
            with act.Fori(3, nblk) as i:
                body(i, i - 1, GU, GU + DN)
            body(nblk, nblk - 1, GU, DN)
            output(nblk - 1, nblk - 1, GU + DN - 1)
            for t in range(NT):
                if t + 1 < NT:
                    act.wait_ge(yt_in[t + 1], 16)
                    act.activation(yt[t + 1][:, 0], yt[t + 1][:, 0], ACT.Copy, scale=gwt[:, 0, t + 1:t + 2]
                                   ).then_inc(fin_w, 1)
                deviation(t, fv, 4 * t + 4, fsd)
                if t + 1 < NT:
                    act.wait_ge(frstd, 3 * t + 3)
                    act.wait_ge(lgv, t + 1)
                    act.activation(ot[t], ot[t], ACT.Copy, scale=rstd[:, t]).then_inc(fin_s, 1)

        @block.vector
        def _(dve):
            def cut(n):
                dve.wait_ge(hi_ready, n + 1)
                dve.tensor_tensor(lo_m[n % HM], raw_m[n % RM], hi_m[n % HM].bitcast(F32), ALU.subtract).then_inc(lo_ready, 1)

            def inverse(t, root, done):
                r = rstd[:, t]
                dve.tensor_scalar(nw[:, t], mv[:, t, 1:2], EPS, None, ALU.add).then_inc(newton, 1)
                dve.wait_ge(root, t + 1)
                dve.reciprocal(r, sd[:, t]).then_inc(newton, 1)
                newton_at[0] += 2
                dve.wait_ge(newton, newton_at[0])
                dve.scalar_tensor_tensor(nw[:, t], nw[:, t], r, r, ALU.mult, ALU.mult).then_inc(done, 1)
                dve.wait_ge(done, 3 * t + 1)
                dve.tensor_scalar(nw[:, t], nw[:, t], -0.5, 1.5, ALU.mult, ALU.add).then_inc(done, 1)
                dve.wait_ge(done, 3 * t + 2)
                dve.tensor_tensor(r, r, nw[:, t], ALU.mult).then_inc(done, 1)

            newton_at = [0]
            conv_at = [0]

            def conv(ops):
                for j, k in ops:
                    t = conv_at[0]
                    w = cwt[:, j, k:k + 1]
                    src = hg[:, j, k:k + S]
                    if k == 0:
                        dve.wait_ge(glu_done, j + 1)
                        dve.wait_ge(cw_ready, 1)
                        dve.wait_ge(pad_zero, 1)
                        dve.tensor_scalar(cacc[:, j], src, w, cwt[:, j, TAPS:TAPS + 1], ALU.mult, ALU.add).then_inc(conv_op, 1)
                    else:
                        dve.wait_ge(conv_op, t - 1)
                        dve.scalar_tensor_tensor(cacc[:, j], src, w, cacc[:, j], ALU.mult, ALU.add).then_inc(conv_op, 1)
                    conv_at[0] += 1

            dve.memset(hg[:, :, 0:TAPS - 1], 0.0).then_inc(pad_zero, 1)
            dve.memset(relb[NBUCKET:NBUCKET + 1], 1.0).then_inc(relb_one, 1)
            for k in range(KT):
                dve.wait_ge(xh_ready, k + 1)
                dve.tensor_tensor(xl[:, k], ps[:, k], xh[:, k].bitcast(F32), ALU.subtract).then_inc(xl_ready, 1)
                if k == 4:
                    cut(0)

            def add_bias(u):
                g, i = divmod(u, NT)
                w = 2 * P if g == 0 and i > 0 else P
                dve.wait_ge(att_s, u + 1)
                if u == 0:
                    dve.wait_ge(bm_in, 96)
                if u >= 2:
                    dve.wait_ge(att_t, u - 1)
                dst = sc[:, u % 2, :, :, 0:w]
                bias = bm12[:, g - 1] if g else bm if w > P else bm[:, :, :, P:2 * P]
                src = ps[:, 2:4, 0:2 * w].rearrange("p a (m w) -> p a m w", m=2)
                dve.tensor_tensor(dst, src, bias, ALU.add).then_inc(s_add, 1)
                dve.wait_ge(s_add, u + 1)
                dve.tensor_reduce(nmx[:, u].rearrange("p (a m) -> p a m", a=2), dst, AX.X, ALU.max, negate=True
                                  ).then_inc(s_max, 1)

            def normalise(u):
                g, i = divmod(u, NT)
                w = 2 * P if g == 0 and i > 0 else P
                dve.wait_ge(att_exp, u + 1)
                dve.reciprocal(rden[:, u], den[:, u]).then_inc(r_den, 1)
                dve.wait_ge(r_den, u + 1)
                v = sc[:, u % 2, :, :, 0:w]
                r = rden[:, u].rearrange("p (a m) -> p a m", a=2).unsqueeze(3).to_broadcast([P, 2, 2, w])
                dve.tensor_tensor(v, v, r, ALU.mult).then_inc(att_p, 1)

            mix_at = [0]

            def mix(ins):
                mix_at[0] += 1
                ins.then_inc(mixv, 1)
                dve.wait_ge(mixv, mix_at[0])

            def merge_lo(d):
                dve.wait_ge(m_hi, d + 1)
                dve.tensor_tensor(xl[:, d], sg1[:, d], xh[:, d].bitcast(F32), ALU.subtract).then_inc(m_ready, 1)

            for s in range(59):
                n, first, last = chunk_of_step(min(s, 57))
                if 1 <= s <= 8 and (s - 1) % 4 >= 2:
                    c = (s - 1) // 4 * 2 + (s - 1) % 4 - 2
                    dve.wait_ge(glu_sig, c + 1)
                    dve.tensor_tensor(hg[:, c, TAPS - 1:], ps[:, s - 3], glu[:, c % 2], ALU.mult).then_inc(glu_done, 1)
                if s in STEP_UNIT:
                    add_bias(STEP_UNIT[s])
                taps = CONV_PLAN.get(s, [])
                conv(taps[:len(taps) // 2])
                if s in STEP_UNIT:
                    normalise(STEP_UNIT[s])
                if s < 42 and first:
                    cut(n + 1)
                conv(taps[len(taps) // 2:])
                if s == 32:
                    dve.wait_ge(ln_den, 1)
                    dve.tensor_tensor(lse, lse, nmx, ALU.subtract).then_inc(lse_ready, 1)
                if s == 34:
                    dve.wait_ge(lse_T, 1)
                    mix(dve.tensor_copy(lsT[:, 0], ps[0:HPG, 2]))
                    for g in (1, 2):
                        mix(dve.tensor_copy(lsT[:, g].rearrange("h (l c) -> h c l", c=4),
                                            ps[0:HPG, 2 + g].rearrange("h (c l) -> h c l", c=4)))
                if s == 35:
                    for t in range(NT):
                        dve.wait_ge(cT_done, t + 1)
                        dve.bn_stats(stats[:, t, 0], ps[:, 4 + t]).then_inc(cstat, 1)
                        dve.wait_ge(cstat, 2 * t + 1)
                        dve.bn_aggr(mv[:, t], stats[:, t, 0]).then_inc(cstat, 1)
                    for t in range(NT):
                        inverse(t, csd, crstd)
                        dve.wait_ge(crstd, 3 * t + 3)
                        dve.tensor_scalar(ctm[:, t], ps[:, 4 + t], mv[:, t, 0:1], rstd[:, t, 0:1], ALU.subtract, ALU.mult
                                          ).then_inc(cnorm, 1)
                if s == 37:
                    mix(dve.tensor_tensor(mxT, lsT[:, 0], lsT[:, 1], ALU.max))
                    mix(dve.tensor_tensor(mxT, mxT, lsT[:, 2], ALU.max))
                    mix(dve.tensor_tensor(lsT, lsT, mxT.unsqueeze(1).to_broadcast([HPG, NG, S]), ALU.subtract))
                    dve.wait_ge(mix_exp, 1)
                    mix(dve.tensor_tensor(mxT, lsT[:, 0], lsT[:, 1], ALU.add))
                    mix(dve.tensor_tensor(mxT, mxT, lsT[:, 2], ALU.add))
                    mix(dve.reciprocal(mxT, mxT))
                    mix(dve.tensor_tensor(lsT, lsT, mxT.unsqueeze(1).to_broadcast([HPG, NG, S]), ALU.mult))
                if s == 39:
                    for j in range(CT):
                        dve.wait_ge(c_hi, j + 1)
                        dve.tensor_tensor(cl[:, j], csil[:, j % 2], ch[:, j].bitcast(F32), ALU.subtract).then_inc(c_ready, 1)
                if s == 41:
                    for m in range(2):
                        for g in range(NG):
                            dve.wait_ge(mix_F, NG * m + g + 1)
                            dve.tensor_tensor(oT[:, g, m], oT[:, g, m], ps[:, 2 + NG * m + g], ALU.mult).then_inc(mixc, 1)
                        dve.wait_ge(mixc, 4 * m + 3)
                        dve.tensor_tensor(oT[:, 0, m], oT[:, 0, m], oT[:, 1, m], ALU.add).then_inc(mixc, 1)
                        dve.wait_ge(mixc, 4 * m + 4)
                        dve.tensor_tensor(oT[:, 0, m], oT[:, 0, m], oT[:, 2, m], ALU.add).then_inc(aT_sum, 1)
                    for m in range(2):
                        dve.wait_ge(aT_hi, m + 1)
                        dve.tensor_tensor(aTl[:, m], oT[:, 0, m], aTh[:, m].bitcast(F32), ALU.subtract).then_inc(aT_ready, 1)
                if 43 <= s <= 50:
                    if s == 43:
                        dve.wait_ge(sig1, 1)
                    dve.wait_ge(proj_done, s)
                    dve.tensor_tensor(sg1[:, s - 43], sg1[:, s - 43], ps[:, (s - 1) % 2], ALU.mult).then_inc(mcv, 1)
                if s in (43, 47, 52):
                    cut(n + 1)
                if s >= 51:
                    if s == 51:
                        dve.wait_ge(sig0, 1)
                    d = s - 51
                    dve.wait_ge(proj_done, s)
                    dve.tensor_tensor(sg0[:, d], sg0[:, d], ps[:, d], ALU.mult).then_inc(mga, 1)
                    dve.wait_ge(mga, d + 1)
                    dve.wait_ge(mcv, d + 1)
                    dve.tensor_tensor(sg1[:, d], sg1[:, d], sg0[:, d], ALU.add).then_inc(merged_sum, 1)
                    if d >= 1:
                        merge_lo(d - 1)
                if s == 57:
                    cut(25)
            merge_lo(KT - 1)
            for n in range(26, NM):
                cut(n)

            def centre(t, rows, par, chain, done):
                dve.wait_ge(chain, 4 * t + 4)
                dve.scalar_tensor_tensor(rows, rows, mv[:, t, 0:1], par[:, 0], ALU.subtract, ALU.mult).then_inc(done, 1)

            def scale(t, rows, par, centred, inv, done):
                dve.wait_ge(centred, t + 1)
                dve.wait_ge(inv, 3 * t + 3)
                dve.scalar_tensor_tensor(rows, rows, rstd[:, t, 0:1], par[:, 1], ALU.mult, ALU.add).then_inc(done, 1)

            def moments(t, rows, chain, at):
                dve.wait_ge(chain, at)
                for h in range(2):
                    dve.bn_stats(stats[:, t, h], rows[:, h * 512:(h + 1) * 512]).then_inc(chain, 1)
                dve.wait_ge(chain, at + 2)
                dve.bn_aggr(mv[:, t], stats[:, t]).then_inc(chain, 1)

            dve.wait_ge(ln_in, 32)
            dve.wait_ge(xr_in, 16)
            for t in range(NT):
                dve.wait_ge(wo_done, t + 1)
                dve.scalar_tensor_tensor(x1[:, t], x1[:, t], ALPHA,
                                         ps[:, 2 * t:2 * t + 2].rearrange("p a c -> p (a c)"),
                                         ALU.mult, ALU.add).then_inc(lnv, 1)
                moments(t, x1[:, t], lnv, 4 * t + 1)
                centre(t, x1[:, t], lnm, lnv, gv)
                inverse(t, lsd, lrstd)
            scale(NT - 1, x1[:, NT - 1], lnm, gv, lrstd, x1_last)

            def cut_e(b, q):
                dve.wait_ge(hi_ready, b * 12 + (NM + q + 1))
                dve.tensor_tensor(lo_e[q % HE], raw_e[q % RE], hi_e[q % HE].bitcast(F32), ALU.subtract).then_inc(lo_ready, 1)

            cut_e(0, 0)

            rv_at = [0]

            def link(ins):
                rv_at[0] += 1
                ins.then_inc(rv, 1)
                dve.wait_ge(rv, rv_at[0])

            def over_e(v):
                return v.unsqueeze(2).to_broadcast([P, NT, NE])

            dve.wait_ge(small_in, 80)
            dve.wait_ge(logits, NT)
            lgp = ps[:, 0:8, 0:NE].rearrange("p (t a) e -> p t a e", a=2)[:, :, 0]
            link(dve.tensor_reduce(c4[:, 0], lgp, AX.X, ALU.max))
            link(dve.tensor_tensor(pr, lgp, over_e(c4[:, 0]), ALU.subtract))
            dve.wait_ge(r_exp, 1)
            link(dve.tensor_reduce(c4[:, 1], pr, AX.X, ALU.add))
            link(dve.reciprocal(c4[:, 1], c4[:, 1]))
            link(dve.tensor_tensor(pr, pr, over_e(c4[:, 1]), ALU.mult))
            p4 = pr.rearrange("p t (g e) -> p (t g) e", e=4)
            link(dve.tensor_tensor(s6[:, :, 0:3], p4[:, :, 0:3], p4[:, :, 1:4], ALU.add))
            link(dve.tensor_tensor(s6[:, :, 3:5], p4[:, :, 0:2], p4[:, :, 2:4], ALU.add))
            link(dve.tensor_tensor(s6[:, :, 5:6], p4[:, :, 0:1], p4[:, :, 3:4], ALU.add))
            link(dve.tensor_reduce(gsc.rearrange("p t g -> p (t g)"), s6, AX.X, ALU.max))

            def first_best(out_, vals, best, cand, n, ids, row):
                bc = lambda v: v.unsqueeze(2).to_broadcast([P, NT, n])
                link(dve.tensor_reduce(c4[:, row], vals, AX.X, ALU.max))
                link(dve.tensor_tensor(cand, vals, bc(c4[:, row]), ALU.is_ge))
                link(dve.scalar_tensor_tensor(cand, cand, -100.0, ids.unsqueeze(1).to_broadcast([P, NT, n]),
                                              ALU.mult, ALU.add))
                link(dve.tensor_reduce(c4[:, best], cand, AX.X, ALU.min))
                link(dve.tensor_tensor(out_, cand, bc(c4[:, best]), ALU.is_equal))

            ids16, ids4 = cst[:, 0:16], cst[:, 24:28]
            first_best(ohg, gsc, 3, gcd, EG, ids4, 2)
            og = ohg.rearrange("p t g -> p (t g)").unsqueeze(2).to_broadcast([P, NT * EG, 4])
            v16 = lambda v: v.rearrange("p t (g e) -> p (t g) e", e=4)
            link(dve.scalar_tensor_tensor(v16(t16a), og, -1.0, p4, ALU.add, ALU.add))
            first_best(oh1, t16a, 3, t16b, NE, ids16, 4)
            link(dve.scalar_tensor_tensor(t16a, oh1, -4.0, t16a, ALU.mult, ALU.add))
            first_best(oh2, t16a, 3, t16b, NE, ids16, 5)
            link(dve.tensor_tensor(sel, oh1, oh2, ALU.add))
            dve.engine_nop().then_inc(sel_ready, 1)
            vte = vt.rearrange("p e t c -> p t e c")
            link(dve.tensor_copy(vte[:, :, :, 0], cst[:, 16:20].unsqueeze(2).to_broadcast([P, NT, NE])))
            link(dve.tensor_tensor(vte[:, :, :, 1], oh2, cst[:, 20:24].unsqueeze(2).to_broadcast([P, NT, NE]), ALU.add))
            dve.wait_ge(rank_mm, 1)
            in_tile = ps[:, 3, 0:NT * NE].rearrange("p (t e) -> p t e", t=NT)
            link(dve.tensor_copy(cum, in_tile))
            for t in range(1, NT):
                link(dve.tensor_tensor(cum[:, t], cum[:, t], cum[:, t - 1], ALU.add))
            link(dve.tensor_tensor(t16a, ps[:, 1, 0:NT * NE].rearrange("p (t e) -> p t e", t=NT), cum, ALU.add))
            link(dve.tensor_tensor(t16a, t16a, in_tile, ALU.subtract))
            link(dve.scalar_tensor_tensor(t16a, t16a, 1.0, sel, ALU.add, ALU.mult))
            link(dve.tensor_scalar(vte[:, :, :, 2], t16a, -1.0, None, ALU.add))
            link(dve.memset(bbase, 0.0))

            def gate_weights():
                link(dve.tensor_tensor(c4[:, 6], c4[:, 4], c4[:, 5], ALU.add))
                link(dve.reciprocal(c4[:, 6], c4[:, 6]))
                link(dve.tensor_tensor(gwt, c4[:, 4:6], c4[:, 6:7].to_broadcast([P, 2, NT]), ALU.mult))

            def block_table():
                cnt = cum[:, NT - 1]
                link(dve.tensor_scalar(xtr, cnt, float(P), None, ALU.is_gt))
                for b in (2, 3):
                    link(dve.scalar_tensor_tensor(xtr, cnt, float(b * P), xtr, ALU.is_gt, ALU.add))
                link(dve.tensor_copy(cs[:, 0], xtr))
                src = 0
                for sh in (1, 2, 4, 8):
                    link(dve.tensor_copy(cs[:, 1 - src, 0:sh], cs[:, src, 0:sh]))
                    link(dve.tensor_tensor(cs[:, 1 - src, sh:], cs[:, src, sh:], cs[:, src, :NE - sh], ALU.add))
                    src = 1 - src
                link(dve.tensor_tensor(cs[:, 1 - src], cs[:, src], xtr, ALU.subtract))
                ends, starts = cs[:, src], cs[:, 1 - src]
                js = cst[:, 28:36].unsqueeze(2).to_broadcast([P, 8, NE])
                row = lambda v: v.unsqueeze(1).to_broadcast([P, 8, NE])
                link(dve.tensor_tensor(ov, js, row(ends), ALU.is_lt))
                link(dve.tensor_tensor(ov2, js, row(starts), ALU.is_ge))
                link(dve.tensor_tensor(ov, ov, ov2, ALU.mult))
                link(dve.tensor_tensor(ov2, js, row(starts), ALU.subtract))
                link(dve.scalar_tensor_tensor(ov2, ov2, 1.0, ov, ALU.add, ALU.mult))
                link(dve.memset(etf, 0.0))
                link(dve.tensor_reduce(bbase[:, NE:NE + 8], ov2, AX.X, ALU.add))
                link(dve.tensor_scalar(bbase[:, NE:NE + 8], bbase[:, NE:NE + 8], float(P), None, ALU.mult))
                link(dve.tensor_tensor(ov, ov, row(ids16), ALU.mult))
                link(dve.tensor_reduce(etf[:, NE:NE + 8], ov, AX.X, ALU.add))
                link(dve.tensor_copy(etf[:, 0:NE], ids16))
                link(dve.tensor_copy(etf[:, TAB - 1:TAB], ends[:, NE - 1:NE]))
                dve.tensor_copy(eti, etf).then_inc(tables, 1)

            bv_at = [0]

            def select(i, static):
                if static:
                    e = i
                else:
                    e = dve.value_load(eti[0:1, bass.ds(i, 1)], min_val=0, max_val=NE - 1)
                dve.tensor_copy(blk, vt[:, bass.ds(e, 1)].rearrange("p a t c -> p (a t) c")).then_inc(bv, 1)
                dve.wait_ge(bv, i * 2 + 1)
                dve.tensor_scalar(blk[:, :, 2], blk[:, :, 2], bbase[:, bass.ds(i, 1)], None, ALU.subtract).then_inc(bv, 1)
                dve.wait_ge(bv, i * 2 + 2)
                for t in range(NT):
                    ins = dve.tensor_scalar(pe_sel[:, t], iota, blk[:, t, 2:3], None, ALU.is_equal)
                ins.then_inc(sel_blk, 1)

            def indices(i):
                dve.wait_ge(idx_mm, i + 1)
                dve.tensor_copy(idf, ps[:, 4, 0:2]).then_inc(idv, 1)
                dve.wait_ge(idv, i * 3 + 1)
                dve.tensor_scalar(idz, idf, 0.0, 8192.0, ALU.is_equal, ALU.mult).then_inc(idv, 1)
                dve.wait_ge(idv, i * 3 + 2)
                dve.scalar_tensor_tensor(idf, idf, -1.0, idz, ALU.add, ALU.add).then_inc(idv, 1)
                dve.wait_ge(idv, i * 3 + 3)
                dve.tensor_copy(orow[:, bass.ds(i, 1)], idf[:, 1:2])
                dve.tensor_copy(gidx, idf[:, 0:1]).then_inc(idx_ready, 1)
                dve.wait_ge(idx_ready, i + 1)

            def output_rows(i):
                if not (isinstance(i, int) and i == 0):
                    dve.wait_ge(y_out, i * 16)
                dve.tensor_copy(sidx, orow[:, bass.ds(i, 1)]).then_inc(sidx_ready, 1)

            def rows_lo(i):
                dve.wait_ge(xeh_ready, i + 1)
                dve.tensor_tensor(xel.rearrange("p k c -> p (k c)"), ps[:, 6:8].rearrange("p a c -> p (a c)"),
                                  xeh.bitcast(F32).rearrange("p k c -> p (k c)"), ALU.subtract).then_inc(xel_ready, 1)

            def hidden_lo(i):
                dve.wait_ge(heh_ready, i + 1)
                dve.tensor_tensor(hel.rearrange("p k c -> p (k c)"), ps[:, 6:8].rearrange("p a c -> p (a c)"),
                                  heh.bitcast(F32).rearrange("p k c -> p (k c)"), ALU.subtract).then_inc(hel_ready, 1)

            def body(i, b, q0, n_chunks, skip=0, prev=True, prev2=True):
                for c in range(skip, n_chunks):
                    cut_e(b, q0 + c)
                    if n_chunks > DN and c == 1:
                        select(i + 1, isinstance(i, int))
                    if c == (2 if n_chunks > DN else 0) and prev:
                        hidden_lo(i - 1)
                    if c == 2 and prev2:
                        output_rows(i - 2)
                    if n_chunks > DN and c == max(2, skip):
                        indices(i + 1)
                    if c == min(GU + 2, n_chunks - 1) and n_chunks > DN:
                        dve.wait_ge(silu_done, i + 1)
                        dve.tensor_tensor(he, he, ps[:, 2:4].rearrange("p a c -> p (a c)"), ALU.mult).then_inc(he_ready, 1)
                        rows_lo(i + 1)

            select(0, True)
            indices(0)
            for m in range(1, HE):
                cut_e(0, m)
            rows_lo(0)
            select(1, True)
            block_table()
            gate_weights()
            body(0, 0, 0, GU, skip=HE, prev=False, prev2=False)
            body(1, 0, GU, GU + DN, prev2=False)
            body(2, 1, GU, GU + DN)
            dve.wait_ge(tables, 1)
            nblk = dve.value_load(eti[0:1, TAB - 1:TAB], min_val=0, max_val=MAXBLK - 1 - NE) + NE
            with dve.Fori(3, nblk) as i:
                body(i, i - 1, GU, GU + DN)
            body(nblk, nblk - 1, GU, DN)
            output_rows(nblk - 1)
            dve.wait_ge(x1_out, 16 * NT)
            dve.tensor_scalar(x1, x1, ALPHA, None, ALU.mult).then_inc(residual, 1)
            dve.wait_ge(residual, 1)
            dve.wait_ge(lnf_in, 32)
            for t in range(NT):
                o = ot[t]
                dve.wait_ge(yt_in[t], 16)
                if t == 0:
                    dve.scalar_tensor_tensor(o, yt[t][:, 0], gwt[:, 0, t:t + 1], x1[:, t], ALU.mult, ALU.add
                                             ).then_inc(fin_0, 1)
                    dve.wait_ge(fin_0, 1)
                else:
                    dve.wait_ge(fin_a, t)
                dve.scalar_tensor_tensor(o, yt[t][:, 1], gwt[:, 1, t:t + 1], o, ALU.mult, ALU.add).then_inc(fv, 1)
                moments(t, o, fv, 4 * t + 1)
                centre(t, o, lnf, fv, lgv)
                inverse(t, fsd, frstd)
            scale(NT - 1, ot[NT - 1], lnf, lgv, frstd, fin_last)


def bucket(dist):
    exact = NBUCKET // 2
    if dist < exact:
        return dist
    v = np.log(np.float32(dist) / np.float32(exact)) / np.float32(math.log(MAXDIST / exact)) * np.float32(NBUCKET - exact)
    return min(exact + int(v), NBUCKET - 1)


def constants():
    sq = np.zeros((5, P, P), np.float32)
    sq[0] = np.eye(P)
    sq[1] = np.triu(np.ones((P, P)), 1)
    sq[2] = np.arange(P)
    sq[3, :, 0:16] = np.arange(16)
    tok = np.arange(NT)[None, :] * P + np.arange(P)[:, None]
    sq[3, :, 16:20] = tok + 1
    sq[3, :, 20:24] = 2 * tok + 1
    sq[3, :, 24:28] = np.arange(4)
    sq[3, :, 28:36] = np.arange(8)
    sq[3, :, 36] = EPS
    for r in range(HPG):
        a, m = divmod(r, 2)
        sq[4, r * 2 + m, a * HD:(a + 1) * HD] = 1.0
    tb = np.zeros((NBUCKET + 1, NG, GTW), np.float32)
    for g, dil in enumerate(DIL):
        for c in range(GTW):
            delta = 2 * P - 1 - c
            if g == 0:
                ok, dist = 0 <= delta <= P, delta
            elif g == 1:
                ok, dist = delta >= 0, delta * dil
            else:
                ok, dist = delta >= 0 and delta % 4 == 0, delta // 4 * dil
            if ok:
                tb[bucket(dist), g, c] = 1.0
            else:
                tb[NBUCKET, g, c] = NEG
    return sq, tb


_INS = ["x", "w_in", "w_attn_out", "w_conv_out", "w_o", "conv_w", "conv_b", "conv_ln_g", "conv_ln_b",
        "ln_mix_g", "ln_mix_b", "expert_w_gate_up", "expert_w_down", "ln_ffn_g", "ln_ffn_b", "router_w", "rel_bias"]


def kernel(**inputs):
    import concourse.bacc as bacc
    from concourse.bass_utils import run_bass_kernel_spmd

    nc = bacc.Bacc("TRN2", target_bir_lowering=False, num_devices=1)
    sq, tb = constants()
    arrays, args = {}, []
    for name, a in [(n, inputs[n]) for n in _INS] + [("c_square", sq), ("c_bucket", tb)]:
        a = np.ascontiguousarray(a)
        arrays[f"in_{name}"] = a
        args.append(nc.dram_tensor(f"in_{name}", a.shape, mybir.dt.from_np(a.dtype), kind="ExternalInput").ap())
    args.append(nc.dram_tensor("out_0", (1, S, D), F32, kind="ExternalOutput").ap())
    build(nc, *args)
    r = run_bass_kernel_spmd(nc, [arrays], core_ids=[0])
    return r.results[0]["out_0"]
```
